# Optimizing a Trainium2 kernel written in Bass

```python
import math
import jax, jax.numpy as jnp
from jax import lax
import numpy as np

D_MODEL = 1024
BATCH = 1
SEQ = 512
DEPTH = 1

D_MIX = 2 * D_MODEL
SSD_INNER = D_MIX // 2
SSD_HEAD_DIM = 64
SSD_HEADS = SSD_INNER // SSD_HEAD_DIM
SSD_GROUPS = 2
SSD_HEADS_PER_GROUP = SSD_HEADS // SSD_GROUPS
SSD_STATE = 128
CONV_WIDTH = 4
CONV_DIM = SSD_INNER + 2 * SSD_GROUPS * SSD_STATE
CHUNK = 128
POOL_WINDOWS = (2, 4, 8, 16)
POOL_WIDTH = D_MIX - SSD_INNER
POOL_GROUP_DIM = POOL_WIDTH // len(POOL_WINDOWS)
IN_PROJ_DIM = SSD_INNER + CONV_DIM + SSD_HEADS + POOL_WIDTH
MEM_LEN = 256
XATTN_HEADS = 4
XATTN_HEAD_DIM = D_MODEL // XATTN_HEADS
D_FF = int(math.ceil((8 * D_MODEL / 3) / 256) * 256)
EPS = 1e-6


def rmsnorm(x, g):
    xf = x.astype(jnp.float32)
    y = xf * lax.rsqrt(jnp.mean(xf * xf, axis=-1, keepdims=True) + EPS)
    return (y * g.astype(jnp.float32)).astype(x.dtype)

def causal_depthwise_conv(u, w, b):
    k, c = w.shape
    out = lax.conv_general_dilated(
        u, w[:, None, :].astype(u.dtype), window_strides=(1,), padding=[(k - 1, 0)],
        dimension_numbers=("NWC", "WIO", "NWC"), feature_group_count=c)
    return out + b.astype(u.dtype)

def ssd_chunked(xs, dt, a, bm, cm):
    bsz, s, _, p = xs.shape
    nc = s // CHUNK
    g, hg, n = SSD_GROUPS, SSD_HEADS_PER_GROUP, SSD_STATE
    xc = (xs * dt[..., None]).reshape(bsz, nc, CHUNK, g, hg, p)
    adt = (dt * a).reshape(bsz, nc, CHUNK, g, hg).transpose(0, 3, 4, 1, 2)
    bc = bm.reshape(bsz, nc, CHUNK, g, n)
    cc = cm.reshape(bsz, nc, CHUNK, g, n)
    a_cs = jnp.cumsum(adt, axis=-1)
    causal = jnp.tril(jnp.ones((CHUNK, CHUNK), dtype=bool))
    seg = jnp.exp(jnp.where(causal, a_cs[..., :, None] - a_cs[..., None, :], -jnp.inf))
    cb = jnp.einsum("bclgn,bcsgn->bgcls", cc, bc)
    y_diag = jnp.einsum("bghcls,bcsghp->bclghp", cb[:, :, None] * seg, xc)
    decay_states = jnp.exp(a_cs[..., -1:] - a_cs)
    states = jnp.einsum("bcsgn,bghcs,bcsghp->bcghpn", bc, decay_states, xc)
    chunk_decay = jnp.exp(a_cs[..., -1])

    def step(carry, inp):
        st, dec = inp
        return dec[..., None, None] * carry + st, carry

    init = jnp.zeros((bsz, g, hg, p, n), jnp.float32)
    _, prev = lax.scan(step, init, (jnp.moveaxis(states, 1, 0), jnp.moveaxis(chunk_decay, -1, 0)))
    y_off = jnp.einsum("bclgn,cbghpn,bghcl->bclghp", cc, prev, jnp.exp(a_cs))
    return (y_diag + y_off).reshape(bsz, s, SSD_HEADS, p)

def multi_scale_pool(v, pool_w, pool_scale):
    bsz, s, _ = v.shape
    vg = v.astype(jnp.float32).reshape(bsz, s, len(POOL_WINDOWS), POOL_GROUP_DIM)
    cs0 = jnp.concatenate([jnp.zeros_like(vg[:, :1]), jnp.cumsum(vg, axis=1)], axis=1)
    pos1 = jnp.arange(1, s + 1, dtype=jnp.float32)
    outs = []
    for gi, w in enumerate(POOL_WINDOWS):
        c = cs0[:, :, gi]
        lower = jnp.pad(c[:, :s + 1 - w], ((0, 0), (w - 1, 0), (0, 0)))
        count = jnp.minimum(pos1, float(w))[None, :, None]
        outs.append((c[:, 1:] - lower) / count - vg[:, :, gi])
    d = jnp.stack(outs, axis=2)
    out = jnp.einsum("bsgc,gcd->bsgd", d, pool_w.astype(jnp.float32)).reshape(bsz, s, POOL_WIDTH)
    return (out * pool_scale.astype(jnp.float32)).astype(v.dtype)

def hybrid_mixer(u, w_in, conv_w, conv_b, dt_bias, a_log, d_skip, ssd_norm, pool_w, pool_scale, w_out):
    bsz, s, _ = u.shape
    proj = u @ w_in
    z, xbc, dt_raw, v = jnp.split(
        proj, [SSD_INNER, SSD_INNER + CONV_DIM, SSD_INNER + CONV_DIM + SSD_HEADS], axis=-1)
    xbc = jax.nn.silu(causal_depthwise_conv(xbc, conv_w, conv_b)).astype(jnp.float32)
    xs, bm, cm = jnp.split(xbc, [SSD_INNER, SSD_INNER + SSD_GROUPS * SSD_STATE], axis=-1)
    xs = xs.reshape(bsz, s, SSD_HEADS, SSD_HEAD_DIM)
    bm = bm.reshape(bsz, s, SSD_GROUPS, SSD_STATE)
    cm = cm.reshape(bsz, s, SSD_GROUPS, SSD_STATE)
    dt = jax.nn.softplus(dt_raw.astype(jnp.float32) + dt_bias.astype(jnp.float32))
    a = -jnp.exp(a_log.astype(jnp.float32))
    y = ssd_chunked(xs, dt, a, bm, cm)
    y = y + d_skip.astype(jnp.float32)[:, None] * xs
    y = y.reshape(bsz, s, SSD_INNER) * jax.nn.silu(z.astype(jnp.float32))
    y_ssd = rmsnorm(y, ssd_norm).astype(u.dtype)
    y_pool = multi_scale_pool(v, pool_w, pool_scale)
    return jnp.concatenate([y_ssd, y_pool], axis=-1) @ w_out

def memory_cross_attention(q_in, m_in, w_q, w_kv, w_o):
    bsz, s, _ = q_in.shape
    q = (q_in @ w_q).reshape(bsz, s, XATTN_HEADS, XATTN_HEAD_DIM)
    k, v = jnp.split(m_in @ w_kv, 2, axis=-1)
    k = k.reshape(bsz, -1, XATTN_HEADS, XATTN_HEAD_DIM)
    v = v.reshape(bsz, -1, XATTN_HEADS, XATTN_HEAD_DIM)
    scores = jnp.einsum("bshd,bmhd->bhsm", q.astype(jnp.float32), k.astype(jnp.float32))
    probs = jax.nn.softmax(scores * (XATTN_HEAD_DIM ** -0.5), axis=-1).astype(v.dtype)
    o = jnp.einsum("bhsm,bmhd->bshd", probs, v).reshape(bsz, s, D_MODEL)
    return o @ w_o

def swiglu(u, w_gate_up, w_down):
    gate, up = jnp.split(u @ w_gate_up, 2, axis=-1)
    return (jax.nn.silu(gate) * up) @ w_down

def first_inputs(seed: int = 0) -> dict:
    key = jax.random.key(seed)
    ks = iter(jax.random.split(key, 32))
    f32 = jnp.float32

    def nrm(shape, fan_in):
        return jax.random.normal(next(ks), shape, f32) * (fan_in ** -0.5)

    def gain(shape):
        return 1.0 + 0.02 * jax.random.normal(next(ks), shape, f32)

    L = DEPTH
    x = jax.random.normal(next(ks), (BATCH, SEQ, D_MODEL), f32)
    mem = jax.random.normal(next(ks), (BATCH, MEM_LEN, D_MODEL), f32)
    dt0 = jnp.exp(jax.random.uniform(next(ks), (L, SSD_HEADS), f32, math.log(1e-3), math.log(1e-1)))
    dt_bias = dt0 + jnp.log(-jnp.expm1(-dt0))
    a_log = jnp.log(jax.random.uniform(next(ks), (L, SSD_HEADS), f32, 1.0, 16.0))
    return {
        "x": x,
        "mem": mem,
        "mix_norm": gain((L, D_MODEL)),
        "w_in": nrm((L, D_MODEL, IN_PROJ_DIM), D_MODEL),
        "conv_w": nrm((L, CONV_WIDTH, CONV_DIM), CONV_WIDTH),
        "conv_b": 0.02 * jax.random.normal(next(ks), (L, CONV_DIM), f32),
        "dt_bias": dt_bias,
        "a_log": a_log,
        "d_skip": gain((L, SSD_HEADS)),
        "ssd_norm": gain((L, SSD_INNER)),
        "pool_w": nrm((L, len(POOL_WINDOWS), POOL_GROUP_DIM, POOL_GROUP_DIM), POOL_GROUP_DIM),
        "pool_scale": gain((L, POOL_WIDTH)),
        "w_out_mix": nrm((L, D_MIX, D_MODEL), D_MIX),
        "xattn_norm": gain((L, D_MODEL)),
        "mem_norm": gain((L, D_MODEL)),
        "w_q": nrm((L, D_MODEL, D_MODEL), D_MODEL),
        "w_kv": nrm((L, D_MODEL, 2 * D_MODEL), D_MODEL),
        "w_o": nrm((L, D_MODEL, D_MODEL), D_MODEL),
        "ffn_norm": gain((L, D_MODEL)),
        "w_gate_up": nrm((L, D_MODEL, 2 * D_FF), D_MODEL),
        "w_down": nrm((L, D_FF, D_MODEL), D_FF),
        "final_norm": gain((D_MODEL,)),
    }

def first_block(x, mem, mix_norm, w_in, conv_w, conv_b, dt_bias, a_log, d_skip, ssd_norm,
              pool_w, pool_scale, w_out_mix, xattn_norm, mem_norm, w_q, w_kv, w_o,
              ffn_norm, w_gate_up, w_down, final_norm):
    h = x
    for l in range(DEPTH):
        h = h + hybrid_mixer(rmsnorm(h, mix_norm[l]), w_in[l], conv_w[l], conv_b[l], dt_bias[l],
                             a_log[l], d_skip[l], ssd_norm[l], pool_w[l], pool_scale[l], w_out_mix[l])
        h = h + memory_cross_attention(rmsnorm(h, xattn_norm[l]), rmsnorm(mem, mem_norm[l]),
                                       w_q[l], w_kv[l], w_o[l])
        h = h + swiglu(rmsnorm(h, ffn_norm[l]), w_gate_up[l], w_down[l])
    return rmsnorm(h, final_norm)


DEPTH_2 = 2

CHUNK_2 = 64
Q_BLOCK = 128
N_MIXERS = 2
HEAD_DIM = 128
N_MEM = 256
MEM_HEADS = 4
MEM_WIDTH = MEM_HEADS * HEAD_DIM
MIX_WIDTH = 2 * D_MODEL
CONV_WIDTH_2 = MIX_WIDTH - MEM_WIDTH
CONV_KERNEL = 31
ATT_HEADS = (MIX_WIDTH - MEM_WIDTH) // HEAD_DIM
ATT_WIDTH = ATT_HEADS * HEAD_DIM
IDX_HEADS = 8
IDX_DIM = 64
TOPK_MAX = 256
ALPHA = (2 * DEPTH_2) ** 0.25
BETA = (8 * DEPTH_2) ** -0.25
LN_EPS = 1e-5
NEG = -1e30

A_SIZES = (2 * CONV_WIDTH_2, MEM_WIDTH, MIX_WIDTH)
B_SIZES = (ATT_WIDTH, HEAD_DIM, HEAD_DIM, IDX_HEADS * IDX_DIM, IDX_DIM, IDX_HEADS, MEM_WIDTH, MIX_WIDTH)
A_IN = sum(A_SIZES)
B_IN = sum(B_SIZES)


def split_cols(h, sizes):
    return jnp.split(h, [int(c) for c in np.cumsum(sizes)[:-1]], axis=-1)

def layer_norm(x, g, b):
    xf = x.astype(jnp.float32)
    mu = xf.mean(-1, keepdims=True)
    var = jnp.square(xf - mu).mean(-1, keepdims=True)
    return ((xf - mu) * lax.rsqrt(var + LN_EPS) * g.astype(jnp.float32) + b.astype(jnp.float32)).astype(x.dtype)

def alibi_slopes(n):
    p = 2 ** int(math.floor(math.log2(n)))
    base = [2.0 ** (-8.0 * (i + 1) / p) for i in range(p)]
    extra = [2.0 ** (-4.0 * (2 * i + 1) / p) for i in range(n - p)]
    return jnp.asarray(base + extra, dtype=jnp.float32)

def mem_cross_attention(q, mem_n, w_mkv):
    B, T, _ = q.shape
    k, v = jnp.split(mem_n @ w_mkv, 2, axis=-1)
    q = q.reshape(B, T, MEM_HEADS, HEAD_DIM)
    k = k.reshape(B, -1, MEM_HEADS, HEAD_DIM)
    v = v.reshape(B, -1, MEM_HEADS, HEAD_DIM)
    s = jnp.einsum('bthd,bnhd->bhtn', q, k).astype(jnp.float32) * (HEAD_DIM ** -0.5)
    p = jax.nn.softmax(s, axis=-1).astype(v.dtype)
    return jnp.einsum('bhtn,bnhd->bthd', p, v).reshape(B, T, MEM_WIDTH)

def conformer_conv(u, conv_w, conv_b, g, b):
    a, gl = jnp.split(u, 2, axis=-1)
    h = a * jax.nn.sigmoid(gl)
    h = jnp.pad(h, ((0, 0), (CONV_KERNEL - 1, 0), (0, 0)))
    h = lax.conv_general_dilated(h, conv_w[:, None, :].astype(h.dtype), (1,), 'VALID',
                                 dimension_numbers=('NWC', 'WIO', 'NWC'),
                                 feature_group_count=CONV_WIDTH_2) + conv_b
    return jax.nn.silu(layer_norm(h, g, b))

def dsa_attention(q, k, v, q_idx, k_idx, w_idx):
    B, T = q.shape[:2]
    topk = min(TOPK_MAX, T // 4)
    nb = T // Q_BLOCK
    slopes = alibi_slopes(ATT_HEADS)
    key_chunk = jnp.arange(T, dtype=jnp.int32) // CHUNK_2
    scale = HEAD_DIM ** -0.5

    def to_blocks(a):
        return jnp.moveaxis(a.reshape(B, nb, Q_BLOCK, *a.shape[2:]), 1, 0)

    def block(args):
        qb, qib, wb, start = args
        qpos = start + jnp.arange(Q_BLOCK, dtype=jnp.int32)
        qchunk = qpos // CHUNK_2
        admiss = key_chunk[None, :] <= qchunk[:, None]
        iscore = jax.nn.relu(jnp.einsum('bqhd,bsd->bqhs', qib, k_idx).astype(jnp.float32))
        iscore = jnp.einsum('bqh,bqhs->bqs', wb.astype(jnp.float32), iscore)
        iscore = jnp.where(admiss[None], iscore, NEG)
        _, sel = lax.top_k(iscore, topk)
        valid = key_chunk[sel] <= qchunk[None, :, None]
        kg = jax.vmap(lambda kb, ib: kb[ib])(k, sel)
        vg = jax.vmap(lambda vb, ib: vb[ib])(v, sel)
        dist = jnp.abs(qpos[None, :, None] - sel).astype(jnp.float32)
        logits = jnp.einsum('bqhd,bqkd->bqhk', qb, kg).astype(jnp.float32) * scale
        logits = logits - slopes[None, None, :, None] * dist[:, :, None, :]
        logits = jnp.where(valid[:, :, None, :], logits, NEG)
        p = jax.nn.softmax(logits, axis=-1).astype(vg.dtype)
        return jnp.einsum('bqhk,bqkd->bqhd', p, vg)

    starts = jnp.arange(nb, dtype=jnp.int32) * Q_BLOCK
    out = lax.map(block, (to_blocks(q), to_blocks(q_idx), to_blocks(w_idx), starts))
    return jnp.moveaxis(out, 0, 1).reshape(B, T, ATT_WIDTH)

def second_inputs(seed: int = 0) -> dict:
    key = jax.random.key(seed)
    ks = jax.random.split(key, 24)
    n_a = (DEPTH_2 + 1) // 2
    n_b = DEPTH_2 // 2
    nrm = lambda k, shape, s: jax.random.normal(k, shape, jnp.float32) * s
    return {
        "x": nrm(ks[0], (BATCH, SEQ, D_MODEL), 1.0),
        "mem": nrm(ks[1], (BATCH, N_MEM, D_MODEL), 1.0),
        "mem_ln_g": 1.0 + nrm(ks[2], (D_MODEL,), 0.05),
        "mem_ln_b": nrm(ks[3], (D_MODEL,), 0.01),
        "a_w_in": nrm(ks[4], (n_a, D_MODEL, A_IN), D_MODEL ** -0.5),
        "a_conv_w": nrm(ks[5], (n_a, CONV_KERNEL, CONV_WIDTH_2), CONV_KERNEL ** -0.5),
        "a_conv_b": nrm(ks[6], (n_a, CONV_WIDTH_2), 0.01),
        "a_ln_g": 1.0 + nrm(ks[7], (n_a, CONV_WIDTH_2), 0.05),
        "a_ln_b": nrm(ks[8], (n_a, CONV_WIDTH_2), 0.01),
        "a_w_mkv": nrm(ks[9], (n_a, D_MODEL, 2 * MEM_WIDTH), D_MODEL ** -0.5),
        "a_w_out": nrm(ks[10], (n_a, MIX_WIDTH, D_MODEL), BETA * MIX_WIDTH ** -0.5),
        "a_post_g": 1.0 + nrm(ks[11], (n_a, D_MODEL), 0.05),
        "a_post_b": nrm(ks[12], (n_a, D_MODEL), 0.01),
        "b_w_in": nrm(ks[13], (n_b, D_MODEL, B_IN), D_MODEL ** -0.5),
        "b_w_mkv": nrm(ks[14], (n_b, D_MODEL, 2 * MEM_WIDTH), D_MODEL ** -0.5),
        "b_w_out": nrm(ks[15], (n_b, MIX_WIDTH, D_MODEL), BETA * MIX_WIDTH ** -0.5),
        "b_post_g": 1.0 + nrm(ks[16], (n_b, D_MODEL), 0.05),
        "b_post_b": nrm(ks[17], (n_b, D_MODEL), 0.01),
    }

def second_block(x, mem, mem_ln_g, mem_ln_b, a_w_in, a_conv_w, a_conv_b, a_ln_g, a_ln_b,
              a_w_mkv, a_w_out, a_post_g, a_post_b, b_w_in, b_w_mkv, b_w_out,
              b_post_g, b_post_b):
    B, T, _ = x.shape
    mem_n = layer_norm(mem, mem_ln_g, mem_ln_b)
    for i in range(DEPTH_2):
        j = i // N_MIXERS
        if i % N_MIXERS == 0:
            u, qm, gate = split_cols(x @ a_w_in[j], A_SIZES)
            y_mix = conformer_conv(u, a_conv_w[j], a_conv_b[j], a_ln_g[j], a_ln_b[j])
            w_mkv, w_out, pg, pb = a_w_mkv[j], a_w_out[j], a_post_g[j], a_post_b[j]
        else:
            q, k, v, qi, ki, wi, qm, gate = split_cols(x @ b_w_in[j], B_SIZES)
            y_mix = dsa_attention(q.reshape(B, T, ATT_HEADS, HEAD_DIM), k, v,
                                  qi.reshape(B, T, IDX_HEADS, IDX_DIM), ki, wi)
            w_mkv, w_out, pg, pb = b_w_mkv[j], b_w_out[j], b_post_g[j], b_post_b[j]
        y_mem = mem_cross_attention(qm, mem_n, w_mkv)
        y = jnp.concatenate([y_mix, y_mem], axis=-1) * jax.nn.silu(gate)
        x = layer_norm(ALPHA * x + y @ w_out, pg, pb)
    return x


def setup_inputs(seed=0):
    out = dict(first_inputs(seed))
    for name, value in second_inputs(seed + 1).items():
        if name != "x":
            out[name + "_2"] = value
    return out


def reference(
    x, mem, mix_norm, w_in, conv_w, conv_b, dt_bias, a_log, d_skip, ssd_norm, pool_w,
    pool_scale, w_out_mix, xattn_norm, mem_norm, w_q, w_kv, w_o, ffn_norm, w_gate_up, w_down,
    final_norm, mem_2, mem_ln_g_2, mem_ln_b_2, a_w_in_2, a_conv_w_2, a_conv_b_2, a_ln_g_2,
    a_ln_b_2, a_w_mkv_2, a_w_out_2, a_post_g_2, a_post_b_2, b_w_in_2, b_w_mkv_2, b_w_out_2,
    b_post_g_2, b_post_b_2,
):
    x = first_block(
        x, mem, mix_norm, w_in, conv_w, conv_b, dt_bias, a_log, d_skip, ssd_norm, pool_w,
        pool_scale, w_out_mix, xattn_norm, mem_norm, w_q, w_kv, w_o, ffn_norm, w_gate_up,
        w_down, final_norm,
    )
    return second_block(
        x, mem_2, mem_ln_g_2, mem_ln_b_2, a_w_in_2, a_conv_w_2, a_conv_b_2, a_ln_g_2, a_ln_b_2,
        a_w_mkv_2, a_w_out_2, a_post_g_2, a_post_b_2, b_w_in_2, b_w_mkv_2, b_w_out_2,
        b_post_g_2, b_post_b_2,
    )


_drawn_inputs = setup_inputs


def setup_inputs(seed=0):
    import zlib

    import numpy as np

    out = dict(_drawn_inputs(seed))
    spreads = {}
    factors = {'conv_b': 2.897,
     'd_skip': 5.67,
     'ssd_norm': 4.102,
     'pool_scale': 4.26,
     'xattn_norm': 8.0,
     'mem_norm': 8.0,
     'ffn_norm': 3.824,
     'mem_2': 3.003,
     'mem_ln_g_2': 8.0,
     'mem_ln_b_2': 8.0,
     'a_conv_b_2': 8.0,
     'a_ln_g_2': 5.576,
     'a_ln_b_2': 8.0,
     'a_w_mkv_2': 3.614,
     'a_post_b_2': 4.059,
     'b_w_mkv_2': 4.921,
     'b_post_b_2': 5.681}
    for name, (base, spread) in spreads.items():
        noise = np.random.default_rng([zlib.crc32(name.encode()), seed]).standard_normal(out[name].shape)
        drawn = base * np.exp(spread * noise) if base else spread * noise
        out[name] = __import__('jax').numpy.asarray(drawn.astype(out[name].dtype))
    for name, factor in factors.items():
        out[name] = (out[name] * factor).astype(out[name].dtype)
    return out
```

```python
from contextlib import ExitStack

import numpy as np
import concourse.bass as bass
from concourse import mybir

ALU = mybir.AluOpType
ACT = mybir.ActivationFunctionType
AX = mybir.AxisListType
F32 = mybir.dt.float32
F32R = mybir.dt.float32r

P = 128
D = 1024
DT = D // P
T = 512
TT = T // P
MEM = 256
MT = MEM // P
KT = 8
WC = 256
EPS = 1e-6
LN_EPS = 1e-5

SSD_INNER = 1024
HEADS = 16
HD = 64
GROUPS = 2
HPG = HEADS // GROUPS
STATE = 128
CONV_DIM = SSD_INNER + 2 * GROUPS * STATE
XT = CONV_DIM // P
XS = SSD_INNER // P
CHUNKS = T // P
WINDOWS = (2, 4, 8, 16)
PAD = 15
D_FF = 2816
XH_ = 4
Z0, XBC0, DT0, V0 = 0, 1024, 2560, 2576

CW = 1536
CT_ = CW // P
TAPS = 31
MH_ = 4
AH = 12
IH = 8
ID = 64
TOPK = 128
ALPHA = 4 ** 0.25
NEG = -1e30
TAKEN = -3.0e38
SLOPES = [2.0 ** -(i + 1) for i in range(8)] + [2.0 ** (-0.5 * (2 * i + 1)) for i in range(4)]


def plan(sizes):
    at, n = {}, 0
    for name, size in sizes:
        at[name] = n
        n += size
    return at, n


FF_CHUNKS = [8, 8, 6]
JOBS, N_JOBS = plan(
    [("kv1_k", 4), ("kv1_v", 4), ("xbc", 6), ("dt", 1), ("v", 4), ("z", 4), ("pool", 1), ("wo_pool", 4),
     ("wo_ssd", 4), ("q1", 4), ("wo1", 4), ("kva_k", 2), ("kva_v", 2)]
    + [x for c, n in enumerate(FF_CHUNKS) for x in ((f"gu{c}", n), (f"down{c}", 4))]
    + [("kvb_k", 2), ("kvb_v", 2), ("a_glu", CT_), ("a_qm", 2), ("a_gate", 8), ("a_out", 8),
       ("b_qi", 2), ("b_k", 1), ("b_v", 1), ("b_q", 6), ("b_qm", 2), ("b_gate", 8), ("b_out", 8)])


def mem_step_tasks(layer, n):
    return ([(f"mv{layer}_{n // 2 - 1}", 1)] if n >= 2 and n % 2 == 0 else []) + \
           ([(f"ms{layer}_{n // 2}", 2)] if n < 8 and n % 2 == 0 else []) + \
           ([(f"mp{layer}_{n // 2}", 2)] if n % 2 else [])


UNITS = [(qb, hg) for qb in range(TT) for hg in range(AH // 4)]


def unit_step_tasks(u):
    return ([(f"bT{u - 1}", UNITS[u - 1][0] + 1)] if u else []) + ([(f"bL{u}", 4)] if u < len(UNITS) else []) + \
           ([(f"bV{u - 1}", 1)] if u else [])


TASKS, N_TASKS = plan(
    [("params", 2), ("mem1", 4), ("x", DT), ("stat1", 1), ("xbcT", XS + GROUPS), ("acs", 1), ("cb", 2), ("abc0", 4)]
    + [t for c in range(CHUNKS) for t in
       ([(f"state{c}", 2)] * (c < CHUNKS - 1) + [(f"yoff{c}", 2)] * (c > 0) + [(f"ydiag{c}", 2)]
        + [(f"abc{c + 1}", 4)] * (c < CHUNKS - 1) + [(f"yT{c}", 2)])]
    + [("stat2", 1)]
    + [t for m in range(TT) for t in ([(f"s1_{m}", 2)] + ([(f"pT1_{m - 1}", 2)] if m else []))] + [(f"pT1_{TT - 1}", 2)]
    + [("pv1", 8), ("mem2", 4), ("stat3", 1), ("stat4", 1)]
    + [t for n in range(9) for t in mem_step_tasks(0, n)] + [("a_mean", 1), ("a_var", 1), ("mean_a", 1), ("var_a", 1)]
    + [("idx", 8 * 3)] + [t for j in range(10) for t in unit_step_tasks(j) + (mem_step_tasks(1, j - 2) if j >= 2 else [])]
    + [t for u in (10, 11, 12) for t in unit_step_tasks(u)] + mem_step_tasks(1, 8)
    + [("mean_b", 1), ("var_b", 1), ("out", 8)])

PARAM_SETS = [
    [("mix_norm", "mix_norm", 8), ("conv_w", "conv_w", 48), ("conv_b", "conv_b", 12), ("ssd_norm", "ssd_norm", 8),
     ("pool_scale", "pool_scale", 8), ("xattn_norm", "xattn_norm", 8), ("mem_norm", "mem_norm", 8),
     ("ffn_norm", "ffn_norm", 8), ("final_norm", "final_norm", 8)],
    [("mem_ln_g", "mem_ln_g_2", 8), ("mem_ln_b", "mem_ln_b_2", 8), ("a_conv_b", "a_conv_b_2", 12),
     ("a_ln_g", "a_ln_g_2", 12), ("a_ln_b", "a_ln_b_2", 12), ("a_post_g", "a_post_g_2", 8),
     ("a_post_b", "a_post_b_2", 8), ("b_post_g", "b_post_g_2", 8), ("b_post_b", "b_post_b_2", 8)],
] + [[(f"a_conv_w{i}", "a_conv_w_2", 124)] for i in range(3)]
SET_ROWS = [sum(r for _, _, r in s) for s in PARAM_SETS]
COL = {}
_c = 0
for _s in PARAM_SETS:
    for _n, _, _r in _s:
        COL[_n] = _c
        _c += _r
N_COLS = _c


def program(nc, A, out):
    with ExitStack() as ctx:
        def sem(name):
            return ctx.enter_context(nc.semaphore(name))

        top = [nc.sbuf_base + 31 & ~31]
        ctx.enter_context(nc.sbuf_tensor("sbuf_map", [P, (nc.sbuf_usable_end - top[0]) // 4 - 16], F32))
        end = nc.sbuf_usable_end

        def at(name, shape, offset, dt=F32):
            return nc.alloc_sbuf_tensor_at(name, shape, dt, offset=offset)

        def region(nbytes):
            o = top[0]
            top[0] = o + (nbytes + 31) // 32 * 32
            assert top[0] <= end, top
            return o

        KB = 1024
        hT = at("hT", [P, DT, T], region(16 * KB))
        w_raw = at("w_raw", [P, 2, KT, WC], region(16 * KB))
        w_hi = at("w_hi", [P, 2, KT, WC], region(16 * KB), F32R)
        w_lo = at("w_lo", [P, 2, KT, WC], region(16 * KB), F32R)
        x_hi = at("x_hi", [P, DT, T], region(16 * KB), F32R)
        x_lo = at("x_lo", [P, DT, T], region(16 * KB), F32R)
        rY = region(48 * KB)
        y_hi = at("y_hi", [P, 12, T], rY, F32R)
        y_lo = at("y_lo", [P, 12, T], rY + 24 * KB, F32R)
        rM = region(16 * KB)
        m_hi = at("m_hi", [P, DT, MEM], rM, F32R)
        m_lo = at("m_lo", [P, DT, MEM], rM + 8 * KB, F32R)
        rK = region(16 * KB)
        k1 = at("k1", [P, DT, MEM], rK)
        v1 = at("v1", [P, MT, D], rK + 8 * KB)
        k_m = [at(f"k_m{i}", [P, MH_, MEM], rK + 8 * KB * i) for i in range(2)]
        v_m = [at(f"v_m{i}", [P, MT, MH_ * P], rK + 8 * KB * i + 4 * KB) for i in range(2)]
        rS = region(41 * KB)
        ident = at("ident", [P, P], region(512))
        ones = at("ones", [P, P], region(512))
        tri = at("tri", [P, P], region(512))
        cols = at("cols", [P, N_COLS], region(4 * N_COLS))
        eps = at("eps", [P, 2], region(8))
        bc = at("bc", [P, 3, HEADS], region(192))
        rSm = region(1856)

        rN = rS + 32 * KB
        rstd = at("rstd", [P, T], rN)
        mean = at("mean", [P, T], rN + 2 * KB)
        nring = at("nring", [P, 2, T], rN + 4 * KB)

        x_nat = at("x_nat", [P, TT, D], rS)
        mem1 = at("mem1", [P, MT, D], rS + 16 * KB)
        p_rows = at("p_rows", [P, 5, P], rS + 24 * KB)
        mstat = at("mstat", [P, 64], rSm)

        ROW = PAD + T + 1
        raw = at("raw", [P, 2, ROW], rS)
        acc = at("acc", [P, 2, ROW], rS + 8 * ROW)
        xdt = at("xdt", [P, HEADS, HD], rS)
        xdd = at("xdd", [P, HEADS, HD], rS + 4 * KB)
        o = rS + 16 * ROW
        zs = at("zs", [P, TT, D], o)
        wbuf = at("wbuf", [P, 2, ROW], rM + 16 * KB - 8 * ROW)
        bT = at("bT", [P, GROUPS, T], o + 16 * KB)
        cT = at("cT", [P, GROUPS, T], o + 20 * KB)
        b_nat = at("b_nat", [P, CHUNKS, GROUPS * STATE], o + 24 * KB)
        cbm = at("cbm", [P, CHUNKS, GROUPS, P], o + 28 * KB)
        assert 16 * ROW + 32 * KB <= 41 * KB
        xs01 = at("xs01", [P, 2, D], rY + 16 * KB)
        xs23 = at("xs23", [P, 2, D], rY + 40 * KB)
        m_ = at("m_", [P, HEADS, P], rM)
        y_nat = at("y_nat", [P, HEADS, HD], rM + 8 * KB)
        prev = at("prev", [P, HEADS, HD], rM + 12 * KB)
        sm = [at(n, [P, CHUNKS, HEADS], rSm + 256 * i) for i, n in
              enumerate(("dt_", "adt", "acs", "eacs", "dtd", "cdec"))]
        dt_, adt, acs, eacs, dtd, cdec = sm
        t1, t2, t3 = [at(n, [P, CHUNKS, HEADS], rM + 8 * KB + 256 * i) for i, n in enumerate(("t1", "t2", "t3"))]
        ysum = at("ysum", [P, 4, 2], rSm + 1536)
        inv_n = at("inv_n", [P, 4, 16], rSm + 1600)

        def xs_nat(c):
            return (xs01 if c < 2 else xs23)[:, c % 2, :]

        qT = at("qT", [P, DT, T], rS)
        pT = at("pT", [P, MT, XH_, T], rS + 16 * KB)
        pr = at("pr", [P, 2, XH_, MEM], rY + 16 * KB)
        mem2 = at("mem2", [P, MT, D], rY + 40 * KB)
        sst = at("sst", [P, TT, 4, XH_], rSm)

        m2ring = at("m2ring", [P, 2, MEM], rS)
        sg = at("sg", [P, 2, T], rS)
        ga = at("ga", [P, 2, T], rS + 4 * KB)

        HP = TAPS - 1
        hc = at("hc", [P, CT_, HP + T], rY)
        ya_lo = at("ya_lo", [P, 8, T], rY + 26112, F32R)
        cacc = at("cacc", [P, 2, T], rY + 26112 + 16 * KB)
        assert CT_ * (HP + T) * 4 <= 26112
        gates = at("gates", [P, 16, T], rS)
        ya_hi = at("ya_hi", [P, 8, T], rS + 16 * KB, F32R)
        qmT = at("qmT", [P, MH_, T], rM)
        prm = at("prm", [P, MH_, MEM], rM + 8 * KB)
        pTm = at("pTm", [P, MT, MH_, P], rM + 12 * KB)
        qB = at("qB", [P, AH, T], rY)
        qiT = at("qiT", [P, IH // 2, T], rY + 24 * KB)
        kB = at("kB", [P, T], rY + 32 * KB)
        kiT = at("kiT", [P, T], rY + 34 * KB)
        vB = at("vB", [P, TT, P], rY + 36 * KB)
        W_OF = [(qb + 1) * P for qb in range(TT)]
        M_AT = [0, P, 3 * P, 6 * P]
        mask = at("mask", [P, 10 * P], rY + 38 * KB)
        I_AT = [None, 0, 2 * P, 5 * P]
        isc = at("isc", [P, 9 * P], rY + 43 * KB)
        wi = at("wi", [P, TT, IH], rY + 43 * KB + 36 * P)
        m8 = at("m8", [P, 8], rY + 43 * KB + 36 * P + 128)
        dist = at("dist", [P, T], rN)
        rring = at("rring", [P, 2, T], rN + 2 * KB)
        pB = at("pB", [P, 4, T], rK)
        pTB = at("pTB", [P, TT, 4 * P], rY + 24 * KB)
        yb_hi = at("yb_hi", [P, 8, T], rY, F32R)
        yb_lo = at("yb_lo", [P, 8, T], rM, F32R)
        onat = at("onat", [P, 2, T], rS)
        dist_i = at("dist_i", [P, T], rN + 6 * KB, mybir.dt.int32)
        ast = at("ast", [P, 13, 3, 4], rSm)
        mst = at("mst", [P, 8, 4, MH_], rSm + 640)

        g_bank = ctx.enter_context(nc.psum_tensor("g_bank", [P, 4, T], F32))
        t_bank = ctx.enter_context(nc.psum_tensor("t_bank", [P, 4, T], F32))

        in_small, in_x, in_mem1, in_mem2 = sem("in_small"), sem("in_x"), sem("in_mem1"), sem("in_mem2")
        in_bc = sem("in_bc")
        w_loaded = [sem("w_loaded0"), sem("w_loaded1")]
        w_taken = sem("w_taken")
        w_split = sem("w_split")
        w_used = sem("w_used")
        g_free = [sem("g_free0"), sem("g_free1")]
        t_ready = sem("t_ready")
        t_free = [sem(f"t_free{i}") for i in range(4)]
        const_ready = sem("const_ready")
        dve_chain, act_chain, pool_chain = sem("dve_chain"), sem("act_chain"), sem("pool_chain")
        cols_ready = sem("cols_ready")
        mem1_sq, mem1_n, m1_hi, m1_lo = sem("mem1_sq"), sem("mem1_n"), sem("m1_hi"), sem("m1_lo")
        h_tile = sem("h_tile")
        sq_ready, sq_used = sem("sq_ready"), sem("sq_used")
        std_ready = sem("std_ready")
        nt_ready, nhi_ready, nlo_ready = sem("nt_ready"), sem("nhi_ready"), sem("nlo_ready")
        k1_ready, v1_ready = sem("k1_ready"), sem("v1_ready")
        pads = sem("pads")
        raw_ready = sem("raw_ready")
        conv_ready, silu_ready = sem("conv_ready"), sem("silu_ready")
        xs_ready = sem("xs_ready")
        dtx, sp_e, sp_l, adt_ready = sem("dtx"), sem("sp_e"), sem("sp_l"), sem("adt_ready")
        ac_ready, ac_exp, small_ready = sem("ac_ready"), sem("ac_exp"), sem("small_ready")
        d_hi, d_lo, d_ready, pool_group = sem("d_hi"), sem("d_lo"), sem("d_ready"), sem("pool_group")
        mvar_root, m2_t = sem("mvar_root"), sem("m2_t")
        yp_hi, yp_lo = sem("yp_hi"), sem("yp_lo")
        zs_ready = sem("zs_ready")
        diff_ready, seg_ready, m_ready = sem("diff_ready"), sem("seg_ready"), sem("m_ready")
        cb_ready = sem("cb_ready")
        xdt_ready, prev_ready, prev_used = sem("xdt_ready"), sem("prev_ready"), sem("prev_used")
        y_ready, ysq_ready, yr_ready, yn_ready = sem("y_ready"), sem("ysq_ready"), sem("yr_ready"), sem("yn_ready")
        ys_hi, ys_lo = sem("ys_hi"), sem("ys_lo")
        h_done = sem("h_done")
        q_ready, mx_ready, e_ready, p_ready, pT_ready = sem("q_ready"), sem("mx_ready"), sem("e_ready"), sem("p_ready"), sem("pT_ready")
        o_hi, o_lo = sem("o_hi"), sem("o_lo")
        mem2_n, m2_hi, m2_lo, mvar = sem("mem2_n"), sem("m2_hi"), sem("m2_lo"), sem("mvar")
        sg_ready, ga_ready, ff_hi, ff_lo = sem("sg_ready"), sem("ga_ready"), sem("ff_hi"), sem("ff_lo")
        kv_ready = sem("kv_ready")
        out_done = [sem("out_done0"), sem("out_done1")]
        kb_used = sem("kb_used")
        glu_s, conv_done, pads_a = sem("glu_s"), sem("conv_done"), sem("pads_a")
        qm_ready, gate_ready = sem("qm_ready"), sem("gate_ready")
        mm_max, mm_exp, mm_prob, mm_pT, mm_o = sem("mm_max"), sem("mm_exp"), sem("mm_prob"), sem("mm_pT"), sem("mm_o")
        mean_ready, cent_ready, csq_ready, csq_used = sem("mean_ready"), sem("cent_ready"), sem("csq_ready"), sem("csq_used")
        root_ready = sem("root_ready")
        cn_ready, cs_ready, yf_ready, yf_hi, yf_lo = sem("cn_ready"), sem("cs_ready"), sem("yf_ready"), sem("yf_hi"), sem("yf_lo")
        b_in, dist_ready = sem("b_in"), sem("dist_ready")
        relu_ready, acc_done = sem("relu_ready"), sem("acc_done")
        um_ready, ue_ready, up_ready, uT_ready, uo_ready = sem("um_ready"), sem("ue_ready"), sem("up_ready"), sem("uT_ready"), sem("uo_ready")
        on_ready, fin_ready = sem("on_ready"), sem("fin_ready")

        col = {n: (lambda c: (lambda k: cols[:, c + k:c + k + 1]))(c) for n, c in COL.items()}

        def w_cols(name, c0, k0=0):
            w = A[name][0]
            return lambda c: w[k0 * P:(k0 + KT) * P, bass.ds(c0 + c, WC)].rearrange("(k p) c -> p k c", p=P)

        block = ctx.enter_context(nc.Block())

        @block.sync
        def _(sp):
            def slot_free(j):
                sp.wait_ge(w_split, j - 1)

            def load(j, par, src, kt=KT, c=(0, WC)):
                h = kt // 2
                for a, b in ((0, h), (h, kt)):
                    sp.dma_start(w_raw[:, par, a:b, c[0]:c[1]], src[:, a:b, :]).then_inc(w_loaded[par], 16)

            def stream(base, n, src, step=WC):
                def one(j, par, c, wait=True):
                    if wait:
                        slot_free(j)
                    load(j, par, src(c))
                if base < 2 or n < 4:
                    for i in range(n):
                        one(base + i, (base + i) % 2, i * step, base + i >= 2)
                    return
                with sp.Fori(0, n // 2) as t:
                    for i in range(2):
                        one(t * 2 + (base + i), (base + i) % 2, t * (2 * step) + i * step)
                for i in range(n // 2 * 2, n):
                    one(base + i, (base + i) % 2, i * step)

            for s, rows in enumerate(PARAM_SETS):
                r = 0
                for name, arr, n in rows:
                    if len(A[arr].shape) == 1:
                        v = A[arr].rearrange("(r c) -> r c", c=P)
                    elif len(A[arr].shape) == 2:
                        v = A[arr].rearrange("a (r c) -> (a r) c", c=P)
                    else:
                        v = A[arr].rearrange("a t (r c) -> (a t r) c", c=P)
                    if s >= 2:
                        v = v[(s - 2) * n:(s - 1) * n, :]
                    sp.dma_start(p_rows[r:r + n, s, :], v).then_inc(in_small, 16)
                    r += n
            sp.dma_start(mem1[:], A["mem"][0].rearrange("(m p) d -> p m d", p=P)).then_inc(in_mem1, 16)
            sp.dma_start(x_nat[:], A["x"][0].rearrange("(m p) d -> p m d", p=P)).then_inc(in_x, 16)
            for i, n in enumerate(("dt_bias", "a_log", "d_skip")):
                sp.dma_start(bc[:, i, :], A[n][0].partition_broadcast(P)).then_inc(in_bc, 16)
            stream(JOBS["kv1_k"], 4, w_cols("w_kv", 0))
            stream(JOBS["kv1_v"], 4, w_cols("w_kv", D))
            stream(JOBS["xbc"], 6, w_cols("w_in", XBC0))
            j = JOBS["dt"]
            slot_free(j)
            load(j, j % 2, A["w_in"][0][:, DT0:DT0 + HEADS].rearrange("(k p) c -> p k c", p=P), c=(0, HEADS))
            stream(JOBS["v"], 4, w_cols("w_in", V0))
            stream(JOBS["z"], 4, w_cols("w_in", Z0))
            j = JOBS["pool"]
            slot_free(j)
            load(j, j % 2, A["pool_w"][0].rearrange("g (k p) c -> p (g k) c", p=P))
            stream(JOBS["wo_pool"], 4, w_cols("w_out_mix", 0, 8))
            stream(JOBS["wo_ssd"], 4, w_cols("w_out_mix", 0))
            stream(JOBS["q1"], 4, w_cols("w_q", 0))
            sp.wait_ge(y_ready, CHUNKS)
            sp.dma_start(mem2[:], A["mem_2"][0].rearrange("(m p) d -> p m d", p=P)).then_inc(in_mem2, 16)
            stream(JOBS["wo1"], 4, w_cols("w_o", 0))
            stream(JOBS["kva_k"], 2, w_cols("a_w_mkv_2", 0))
            stream(JOBS["kva_v"], 2, w_cols("a_w_mkv_2", MH_ * P))
            f0 = 0
            for c, n in enumerate(FF_CHUNKS):
                gu = A["w_gate_up"][0].rearrange("(k p) c -> p k c", p=P)
                base = JOBS[f"gu{c}"]
                with sp.Fori(0, n // 2) as t:
                    for i in range(2):
                        par = (base + i) % 2
                        slot_free(t * 2 + (base + i))
                        for h in range(2):
                            src = gu[:, :, bass.ds(t * (2 * P) + (h * D_FF + (f0 + i) * P), P)]
                            sp.dma_start(w_raw[:, par, :, h * P:(h + 1) * P], src).then_inc(w_loaded[par], 16)
                base = JOBS[f"down{c}"]
                dn = A["w_down"][0][f0 * P:(f0 + n) * P, :].rearrange("(k p) c -> p k c", p=P)
                with sp.Fori(0, 2) as t:
                    for i in range(2):
                        slot_free(t * 2 + (base + i))
                        load(None, (base + i) % 2, dn[:, :, bass.ds(t * (2 * WC) + i * WC, WC)], kt=n)
                f0 += n
            stream(JOBS["kvb_k"], 2, w_cols("b_w_mkv_2", 0))
            stream(JOBS["kvb_v"], 2, w_cols("b_w_mkv_2", MH_ * P))
            base = JOBS["a_glu"]
            aw = A["a_w_in_2"][0].rearrange("(k p) c -> p k c", p=P)
            with sp.Fori(0, CT_ // 2) as t:
                for i in range(2):
                    par = (base + i) % 2
                    slot_free(t * 2 + (base + i))
                    for h in range(2):
                        sp.dma_start(w_raw[:, par, :, h * P:(h + 1) * P], aw[:, :, bass.ds(t * (2 * P) + (h * CW + i * P), P)]).then_inc(w_loaded[par], 16)
            stream(JOBS["a_qm"], 2, w_cols("a_w_in_2", 2 * CW))
            g0 = 2 * CW + MH_ * P
            stream(JOBS["a_gate"], 2, w_cols("a_w_in_2", g0 + CT_ * P))
            stream(JOBS["a_gate"] + 2, 6, w_cols("a_w_in_2", g0))
            for h in range(2):
                stream(JOBS["a_out"] + 4 * h, 4, w_cols("a_w_out_2", 0, 8 * h))
            o = np.cumsum([0, AH * P, P, P, IH * ID, ID, IH, MH_ * P])
            stream(JOBS["b_qi"], 2, w_cols("b_w_in_2", int(o[3])))
            bw = A["b_w_in_2"][0].rearrange("(k p) c -> p k c", p=P)
            j = JOBS["b_k"]
            slot_free(j)
            for n, (c0, src, w) in enumerate(((0, int(o[1]), P), (P, int(o[4]), ID), (P + ID, int(o[4]), ID))):
                sp.dma_start(w_raw[:, j % 2, :, c0:c0 + w], bw[:, :, src:src + w]).then_inc(w_loaded[j % 2], 16)
            j = JOBS["b_v"]
            slot_free(j)
            for n, (c0, src, w) in enumerate(((0, int(o[2]), P), (P, int(o[5]), IH))):
                sp.dma_start(w_raw[:, j % 2, :, c0:c0 + w], bw[:, :, src:src + w]).then_inc(w_loaded[j % 2], 16)
            stream(JOBS["b_q"], 6, w_cols("b_w_in_2", 0))
            stream(JOBS["b_qm"], 2, w_cols("b_w_in_2", int(o[6])))
            stream(JOBS["b_gate"], 8, w_cols("b_w_in_2", int(o[7])))
            for h in range(2):
                stream(JOBS["b_out"] + 4 * h, 4, w_cols("b_w_out_2", 0, 8 * h))
            for i in range(8):
                sp.wait_ge(on_ready, i + 1)
                m, h = i // 2, i % 2
                sp.dma_start(out[0, m * P:(m + 1) * P, h * T:(h + 1) * T], onat[:, i % 2, :]).then_inc(out_done[i % 2], 16)
            for done_sem in out_done:
                sp.wait_ge(done_sem, 16 * 4)

        @block.gpsimd
        def _(pool):
            pool_n = [0]

            def link(ins):
                pool_n[0] += 1
                ins.then_inc(pool_chain, 1)
                pool.wait_ge(pool_chain, pool_n[0])

            link(nc.gpsimd.memset(ident[:], 0.0))
            link(nc.gpsimd.affine_select(out=ident[:], in_=ident[:], compare_op=ALU.not_equal, fill=1.0, base=0,
                                         pattern=[[-1, P]], channel_multiplier=1))
            link(nc.gpsimd.memset(ones[:], 1.0))
            link(nc.gpsimd.affine_select(out=tri[:], in_=ones[:], compare_op=ALU.is_ge, fill=0.0, base=0,
                                         pattern=[[1, P]], channel_multiplier=-1))
            link(nc.gpsimd.memset(eps[:, 0:1], EPS))
            for i, w in enumerate(WINDOWS):
                link(nc.gpsimd.memset(inv_n[:, i, :], 1.0 / w))
                for t in range(w - 1):
                    ins = nc.gpsimd.memset(inv_n[:, i, t:t + 1], 1.0 / (t + 1))
            link(ins)
            nc.gpsimd.memset(eps[:, 1:2], LN_EPS).then_inc(const_ready, 1)

            def split(par):
                nc.gpsimd.tensor_scalar(w_hi[:, par], w_raw[:, par], 1.0, 0.0, ALU.mult, ALU.add).then_inc(pool_chain, 1)

            n0 = pool_n[0]

            def job(j, par, loads, used):
                pool.wait_ge(w_loaded[par], loads)
                if used is not None:
                    pool.wait_ge(w_used, used)
                    pool.nop().then_inc(w_taken, 1)
                split(par)
                pool.wait_ge(pool_chain, j + (n0 + 1))
                for q in range(4):
                    s = slice(2 * q, 2 * q + 2)
                    last = nc.gpsimd.tensor_tensor(w_lo[:, par, s], w_raw[:, par, s], w_hi[:, par, s].bitcast(F32), ALU.subtract)
                last.then_inc(w_split, 1)

            for j in range(2):
                job(j, j, 32, None)
            odd = JOBS["b_k"]
            assert odd % 2 == 0 and N_JOBS % 2 == 0
            with pool.Fori(1, odd // 2) as t:
                for i in range(2):
                    job(t * 2 + i, i, t * 32 + 32, t * 2 + (i - 1))
            pool.wait_ge(nlo_ready, 5 * DT)
            nc.gpsimd.iota(dist_i[:], pattern=[[-1, T]], base=T - P, channel_multiplier=1).then_inc(dist_ready, 1)
            with pool.Fori(odd // 2, N_JOBS // 2) as t:
                for i in range(2):
                    job(t * 2 + i, i, t * 32 + (32 + 16 * (i == 0)), t * 2 + (i - 1))

        @block.tensor
        def _(pe):
            def slot(j, par, free):
                pe.wait_ge(w_split, j + 1)
                if free is not None:
                    pe.wait_ge(g_free[par], free)

            def products_T(par, hi, lo, kt=KT, n=T, k0=0, x0=0, pair=None):
                pair = par if pair is None else pair
                for f in range(2):
                    for k in range(kt):
                        ws = slice(f * P, (f + 1) * P)
                        for q, (ww, xx) in enumerate(((w_hi, hi), (w_hi, lo), (w_lo, hi))):
                            xk = xx(x0 + k) if callable(xx) else xx[:, x0 + k, 0:n]
                            last = nc.tensor.matmul(g_bank[:, 2 * pair + f, 0:n], ww[:, par, k0 + k, ws], xk,
                                                    start=(k == 0 and q == 0), stop=(k == kt - 1 and q == 2))
                return last

            def products_as_ready(j, hi, lo, wait, kt=KT, k0=0):
                par = j % 2
                slot(j, par, j // 2)
                for k in range(kt):
                    wait(k)
                    for f in range(2):
                        ws = slice(f * P, (f + 1) * P)
                        for q, (ww, xx) in enumerate(((w_hi, hi), (w_hi, lo), (w_lo, hi))):
                            last = nc.tensor.matmul(g_bank[:, 2 * par + f, :], ww[:, par, k, ws], xx[:, k0 + k, :],
                                                    start=(k == 0 and q == 0), stop=(k == kt - 1 and q == 2))
                last.then_inc(w_used, 1)

            def products_nat(par, hi, lo, mt, n=WC):
                for m in range(mt):
                    for k in range(KT):
                        for q, (xx, ww) in enumerate(((hi, w_hi), (hi, w_lo), (lo, w_hi))):
                            last = nc.tensor.matmul(g_bank[:, 2 * par + m // 2, m % 2 * WC:m % 2 * WC + n],
                                                    xx[:, k, m * P:(m + 1) * P], ww[:, par, k, 0:n],
                                                    start=(k == 0 and q == 0), stop=(k == KT - 1 and q == 2))
                return last

            def jobs(base, n, work):
                def one(j, par, free):
                    slot(j, par, free)
                    work(par).then_inc(w_used, 1)
                if base < 2 or n < 4:
                    for i in range(n):
                        j = base + i
                        one(j, j % 2, j // 2 if j >= 2 else None)
                    return
                with pe.Fori(0, n // 2) as t:
                    for i in range(2):
                        one(t * 2 + (base + i), (base + i) % 2, t + (base + i) // 2)
                for i in range(n // 2 * 2, n):
                    one(base + i, (base + i) % 2, (base + i) // 2)

            def bank(i):
                if i >= 4:
                    pe.wait_ge(t_free[i % 4], i // 4)
                return t_bank[:, i % 4, :]

            def statistic(i, n, src, base, used):
                b = bank(i)
                for k in range(n):
                    pe.wait_ge(base[0], base[1] + k + 1)
                    last = nc.tensor.matmul(b, ones[:], src(k), start=(k == 0), stop=(k == n - 1))
                    if used is not None and k < n - 1:
                        last.then_inc(used, 1)
                last.then_inc(t_ready, 1)

            def sq(k):
                return nring[:, k % 2, :]

            pe.wait_ge(const_ready, 1)
            pe.wait_ge(in_small, 16 * sum(len(s) for s in PARAM_SETS))
            b = bank(0)
            for s in range(4):
                n = SET_ROWS[s]
                last = nc.tensor.transpose(b[:, s * P:s * P + n], p_rows[0:n, s, :], ident[0:n, 0:n])
            last.then_inc(t_ready, 1)
            b = bank(1)
            n = SET_ROWS[4]
            nc.tensor.transpose(b[:, 0:n], p_rows[0:n, 4, :], ident[0:n, 0:n]).then_inc(t_ready, 1)
            pe.wait_ge(mem1_n, MT)
            for i in range(4):
                b = bank(TASKS["mem1"] + i)
                for kk in range(2):
                    for m in range(MT):
                        last = nc.tensor.transpose(b[:, kk * MEM + m * P:kk * MEM + (m + 1) * P],
                                                   mem1[:, m, (2 * i + kk) * P:(2 * i + kk + 1) * P], ident[:])
                last.then_inc(t_ready, 1)
            pe.wait_ge(in_x, 16)
            for k in range(DT):
                b = bank(TASKS["x"] + k)
                for m in range(TT):
                    last = nc.tensor.transpose(b[:, m * P:(m + 1) * P], x_nat[:, m, k * P:(k + 1) * P], ident[:])
                last.then_inc(t_ready, 1)
            statistic(TASKS["stat1"], DT, sq, (sq_ready, 0), sq_used)
            pe.wait_ge(m1_lo, DT)
            jobs(JOBS["kv1_k"], 4, lambda par: products_T(par, m_hi, m_lo, n=MEM))
            jobs(JOBS["kv1_v"], 4, lambda par: products_nat(par, m_hi, m_lo, MT))

            def xbc_T(i):
                pe.wait_ge(silu_ready, i + 1)
                b = bank(TASKS["xbcT"] + i)
                src = acc[:, i % 2, 0:T] if i < XS else bT[:, i - XS, :]
                for c in range(CHUNKS):
                    last = nc.tensor.transpose(b[:, c * P:(c + 1) * P], src[:, c * P:(c + 1) * P], ident[:])
                last.then_inc(t_ready, 1)

            for i in range(XT // 2):
                if i:
                    jobs(JOBS["xbc"] + i, 1, lambda par: products_T(par, x_hi, x_lo))
                else:
                    products_as_ready(JOBS["xbc"], x_hi, x_lo, lambda k: pe.wait_ge(nlo_ready, k + 1))
                if i:
                    for q in range(2):
                        xbc_T(2 * (i - 1) + q)
            jobs(JOBS["dt"], 1, lambda par: products_nat(par, x_hi, x_lo, TT, n=HEADS))
            with_v = JOBS["v"]
            jobs(with_v, 2, lambda par: products_T(par, x_hi, x_lo))
            pe.wait_ge(adt_ready, 1)
            b = bank(TASKS["acs"])
            nc.tensor.matmul(b[:, 0:64], tri[:], adt[:].rearrange("p c h -> p (c h)"), start=True, stop=True)
            nc.tensor.matmul(b[:, 64:128], ones[:], adt[:].rearrange("p c h -> p (c h)"), start=True, stop=True).then_inc(t_ready, 1)
            jobs(with_v + 2, 2, lambda par: products_T(par, x_hi, x_lo))
            def a_bc(c):
                for q in range(4):
                    b = bank(TASKS[f"abc{c}"] + q)
                    for i in range(4):
                        h = 4 * q + i
                        last = nc.tensor.matmul(b[:, i * P:(i + 1) * P], adt[:, c, h:h + 1].to_broadcast([P, P]), tri[:],
                                                start=True, stop=True)
                    last.then_inc(t_ready, 1)

            jobs(JOBS["z"], 2, lambda par: products_nat(par, x_hi, x_lo, TT))
            pe.wait_ge(silu_ready, XT)
            for i in range(2):
                b = bank(TASKS["cb"] + i)
                for q in range(4):
                    c, g = (4 * i + q) // GROUPS, q % GROUPS
                    last = nc.tensor.matmul(b[:, q * P:(q + 1) * P], bT[:, g, c * P:(c + 1) * P], cT[:, g, c * P:(c + 1) * P],
                                            start=True, stop=True)
                last.then_inc(t_ready, 1)
            a_bc(0)
            jobs(JOBS["z"] + 2, 2, lambda par: products_nat(par, x_hi, x_lo, TT))
            j = JOBS["pool"]
            slot(j, j % 2, j // 2)
            for g in range(4):
                if g == 0:
                    pe.wait_ge(g_free[(j + 1) % 2], (j + 1) // 2)
                if g >= 2:
                    pe.wait_ge(yp_lo, 2 * g - 2)
                pe.wait_ge(d_lo, 2 * g + 2)
                last = products_T(j % 2, y_hi, y_lo, kt=2, k0=2 * g, x0=2 * g, pair=(j + 1 + g) % 2)
                last.then_inc(pool_group, 1)
            pe.wait_ge(yp_lo, 8)
            pe.nop().then_inc(w_used, 1)
            for c in range(CHUNKS):
                pe.wait_ge(xdt_ready, c + 1)
                if c < CHUNKS - 1:
                    for g in range(GROUPS):
                        b = bank(TASKS[f"state{c}"] + g)
                        nc.tensor.matmul(b, b_nat[:, c, g * STATE:(g + 1) * STATE], xdd[:, g * HPG:(g + 1) * HPG, :],
                                         start=True, stop=True).then_inc(t_ready, 1)
                if c:
                    pe.wait_ge(prev_ready, c)
                    for g in range(GROUPS):
                        b = bank(TASKS[f"yoff{c}"] + g)
                        nc.tensor.matmul(b, cT[:, g, c * P:(c + 1) * P], prev[:, g * HPG:(g + 1) * HPG, :],
                                         start=True, stop=True).then_inc(t_ready, 1)
                pe.wait_ge(m_ready, c + 1)
                for g in range(GROUPS):
                    b = bank(TASKS[f"ydiag{c}"] + g)
                    for i in range(HPG):
                        h = g * HPG + i
                        last = nc.tensor.matmul(b[:, i * HD:(i + 1) * HD], m_[:, h, :], xdt[:, h, :], start=True, stop=True)
                    last.then_inc(t_ready, 1)
                if c < CHUNKS - 1:
                    a_bc(c + 1)
                jobs(JOBS["wo_pool"] + c, 1, lambda par: products_T(par, y_hi, y_lo))
                pe.wait_ge(yn_ready, c + 1)
                yv = y_nat[:].rearrange("p h d -> p (h d)")
                for g in range(2):
                    b = bank(TASKS[f"yT{c}"] + g)
                    for q in range(4):
                        k = 4 * g + q
                        last = nc.tensor.transpose(b[:, q * P:(q + 1) * P], yv[:, k * P:(k + 1) * P], ident[:])
                    last.then_inc(t_ready, 1)
            products_as_ready(JOBS["wo_ssd"], x_hi, x_lo, lambda k: pe.wait_ge(ys_lo, 8 * (CHUNKS - 1) + k + 1))
            jobs(JOBS["wo_ssd"] + 1, 4 - 1, lambda par: products_T(par, x_hi, x_lo))
            statistic(TASKS["stat2"], DT, sq, (sq_ready, 8), sq_used)
            products_as_ready(JOBS["q1"], x_hi, x_lo, lambda k: pe.wait_ge(nlo_ready, DT + k + 1))
            jobs(JOBS["q1"] + 1, 4 - 1, lambda par: products_T(par, x_hi, x_lo))
            pe.wait_ge(q_ready, DT)
            pe.wait_ge(v1_ready, 4)

            def p_T(m):
                pe.wait_ge(p_ready, m + 1)
                for mm in range(MT):
                    b = bank(TASKS[f"pT1_{m}"] + mm)
                    for h in range(XH_):
                        last = nc.tensor.transpose(b[:, h * P:(h + 1) * P], pr[:, m % 2, h, mm * P:(mm + 1) * P], ident[:])
                    last.then_inc(t_ready, 1)

            for m in range(TT):
                for q in range(2):
                    b = bank(TASKS[f"s1_{m}"] + q)
                    for i in range(2):
                        h = 2 * q + i
                        for kk in range(2):
                            last = nc.tensor.matmul(b[:, i * MEM:(i + 1) * MEM], qT[:, 2 * h + kk, m * P:(m + 1) * P],
                                                    k1[:, 2 * h + kk, :], start=(kk == 0), stop=(kk == 1))
                    last.then_inc(t_ready, 1)
                if m:
                    p_T(m - 1)
            p_T(TT - 1)
            pe.wait_ge(pT_ready, MT * TT)
            for i in range(8):
                b = bank(TASKS["pv1"] + i)
                for mm in range(MT):
                    last = nc.tensor.matmul(b, v1[:, mm, i * P:(i + 1) * P], pT[:, mm, i // 2, :], start=(mm == 0), stop=(mm == 1))
                last.then_inc(t_ready, 1)
            products_as_ready(JOBS["wo1"], y_hi, y_lo, lambda k: pe.wait_ge(o_lo, k + 1))
            pe.wait_ge(mem2_n, MT)
            for i in range(4):
                b = bank(TASKS["mem2"] + i)
                for kk in range(2):
                    for m in range(MT):
                        last = nc.tensor.transpose(b[:, kk * MEM + m * P:kk * MEM + (m + 1) * P],
                                                   mem2[:, m, (2 * i + kk) * P:(2 * i + kk + 1) * P], ident[:])
                last.then_inc(t_ready, 1)
            jobs(JOBS["wo1"] + 1, 3, lambda par: products_T(par, y_hi, y_lo))
            statistic(TASKS["stat3"], DT, sq, (sq_ready, 16), sq_used)
            pe.wait_ge(m2_lo, DT)
            jobs(JOBS["kva_k"], 2, lambda par: products_T(par, m_hi, m_lo, n=MEM))
            jobs(JOBS["kva_v"], 2, lambda par: products_nat(par, m_hi, m_lo, MT))
            products_as_ready(JOBS["gu0"], x_hi, x_lo, lambda k: pe.wait_ge(nlo_ready, 2 * DT + k + 1))
            f0 = 0
            for c, n in enumerate(FF_CHUNKS):
                first = 1 if c == 0 else 0
                jobs(JOBS[f"gu{c}"] + first, n - first, lambda par: products_T(par, x_hi, x_lo))
                products_as_ready(JOBS[f"down{c}"], y_hi, y_lo, lambda k: pe.wait_ge(ff_lo, f0 + k + 1), kt=n)
                jobs(JOBS[f"down{c}"] + 1, 3, lambda par: products_T(par, y_hi, y_lo, kt=n))
                f0 += n
            statistic(TASKS["stat4"], DT, sq, (sq_ready, 24), sq_used)
            jobs(JOBS["kvb_k"], 2, lambda par: products_T(par, m_hi, m_lo, n=MEM))
            jobs(JOBS["kvb_v"], 2, lambda par: products_nat(par, m_hi, m_lo, MT))

            products_as_ready(JOBS["a_glu"], x_hi, x_lo, lambda k: pe.wait_ge(nlo_ready, 3 * DT + k + 1))
            jobs(JOBS["a_glu"] + 1, CT_ - 1, lambda par: products_T(par, x_hi, x_lo))
            jobs(JOBS["a_qm"], 2, lambda par: products_T(par, x_hi, x_lo))

            def mem_step(layer, n):
                kT, vn = k_m[layer], v_m[layer]
                if n >= 2 and n % 2 == 0:
                    m = n // 2 - 1
                    pe.wait_ge(mm_pT, 8 * layer + 2 * m + 2)
                    b = bank(TASKS[f"mv{layer}_{m}"])
                    for h in range(MH_):
                        for mm in range(MT):
                            last = nc.tensor.matmul(b[:, h * P:(h + 1) * P], vn[:, mm, h * P:(h + 1) * P], pTm[:, mm, h, :],
                                                    start=(mm == 0), stop=(mm == 1))
                    last.then_inc(t_ready, 1)
                if n < 8 and n % 2 == 0:
                    m = n // 2
                    pe.wait_ge(qm_ready, 2 * layer + 2)
                    for q in range(2):
                        b = bank(TASKS[f"ms{layer}_{m}"] + q)
                        for i in range(2):
                            h = 2 * q + i
                            last = nc.tensor.matmul(b[:, i * MEM:(i + 1) * MEM], qmT[:, h, m * P:(m + 1) * P], kT[:, h, :],
                                                    start=True, stop=True)
                        last.then_inc(t_ready, 1)
                if n % 2:
                    m = n // 2
                    pe.wait_ge(mm_prob, 4 * layer + m + 1)
                    for mm in range(MT):
                        b = bank(TASKS[f"mp{layer}_{m}"] + mm)
                        for h in range(MH_):
                            last = nc.tensor.transpose(b[:, h * P:(h + 1) * P], prm[:, h, mm * P:(mm + 1) * P], ident[:])
                        last.then_inc(t_ready, 1)

            for n in range(8):
                jobs(JOBS["a_gate"] + n, 1, lambda par: products_T(par, x_hi, x_lo))
                mem_step(0, n)
            mem_step(0, 8)
            statistic(TASKS["a_mean"], CT_, lambda k: hc[:, k, HP:HP + T], (conv_done, 0), None)
            statistic(TASKS["a_var"], CT_, sq, (csq_ready, 0), csq_used)
            products_as_ready(JOBS["a_out"], x_hi, x_lo, lambda k: pe.wait_ge(yf_lo, 4 + k + 1))
            jobs(JOBS["a_out"] + 1, 4 - 1, lambda par: products_T(par, x_hi, x_lo))
            products_as_ready(JOBS["a_out"] + 4, ya_hi, ya_lo, lambda k: pe.wait_ge(yf_lo, min(12 + k + 1, 16)))
            jobs(JOBS["a_out"] + 5, 3, lambda par: products_T(par, ya_hi, ya_lo))

            def layer_norm_stats(name, layer):
                statistic(TASKS[f"mean_{name}"], DT, lambda k: hT[:, k, :], (h_done, 48 + 16 * layer + 8), None)
                statistic(TASKS[f"var_{name}"], DT, sq, (csq_ready, CT_ + DT * layer), csq_used)

            layer_norm_stats("a", 0)
            products_as_ready(JOBS["b_qi"], x_hi, x_lo, lambda k: pe.wait_ge(nlo_ready, 4 * DT + k + 1))
            jobs(JOBS["b_qi"] + 1, 2 - 1, lambda par: products_T(par, x_hi, x_lo))
            jobs(JOBS["b_k"], 1, lambda par: products_T(par, x_hi, x_lo))
            jobs(JOBS["b_v"], 1, lambda par: products_nat(par, x_hi, x_lo, TT, n=P + IH))
            pe.wait_ge(b_in, 3)
            for n in range(6):
                jobs(JOBS["b_q"] + n, 1, lambda par: products_T(par, x_hi, x_lo))
                for i in range(4 * n, 4 * n + 4):
                    qb, h = 1 + i // IH, i % IH
                    b = bank(TASKS["idx"] + i)
                    r = slice(ID * (h % 2), ID * (h % 2) + ID)
                    nc.tensor.matmul(b[:, 0:W_OF[qb]], qiT[r, h // 2, qb * P:(qb + 1) * P], kiT[r, 0:W_OF[qb]],
                                     start=True, stop=True).then_inc(t_ready, 1)

            def unit_step(u):
                if u:
                    qb, hg = UNITS[u - 1]
                    pe.wait_ge(up_ready, u)
                    for kt in range(qb + 1):
                        b = bank(TASKS[f"bT{u - 1}"] + kt)
                        for i in range(4):
                            last = nc.tensor.transpose(b[:, i * P:(i + 1) * P], pB[:, i, kt * P:(kt + 1) * P], ident[:])
                        last.then_inc(t_ready, 1)
                if u < len(UNITS):
                    qb, hg = UNITS[u]
                    if u == 0:
                        pe.wait_ge(b_in, 9)
                    for i in range(4):
                        b = bank(TASKS[f"bL{u}"] + i)
                        nc.tensor.matmul(b[:, 0:W_OF[qb]], qB[:, 4 * hg + i, qb * P:(qb + 1) * P], kB[:, 0:W_OF[qb]],
                                         start=True, stop=True).then_inc(t_ready, 1)
                if u:
                    qb, hg = UNITS[u - 1]
                    b = bank(TASKS[f"bV{u - 1}"])
                    n_T = sum(UNITS[x][0] + 1 for x in range(u))
                    pe.wait_ge(uT_ready, n_T)
                    for kt in range(qb + 1):
                        last = nc.tensor.matmul(b, vB[:, kt, :], pTB[:, kt, :], start=(kt == 0), stop=(kt == qb))
                    last.then_inc(t_ready, 1)

            for n in range(10):
                jobs((JOBS["b_qm"] + n), 1, lambda par: products_T(par, x_hi, x_lo))
                unit_step(n)
                if n >= 2:
                    mem_step(1, n - 2)
            for u in (10, 11, 12):
                unit_step(u)
            mem_step(1, 8)
            pe.wait_ge(yf_lo, 24)
            jobs(JOBS["b_out"], 4, lambda par: products_T(par, x_hi, x_lo))
            pe.wait_ge(yf_lo, 32)
            jobs(JOBS["b_out"] + 4, 4, lambda par: products_T(par, lambda k: yb_hi[:, k, :], lambda k: yb_lo[:, (k + 4) % 8, :]))
            layer_norm_stats("b", 1)
            for i in range(8):
                m, h = i // 2, i % 2
                pe.wait_ge(fin_ready, 4 * h + 4)
                b = bank(TASKS["out"] + i)
                for q in range(4):
                    last = nc.tensor.transpose(b[:, q * P:(q + 1) * P], hT[:, 4 * h + q, m * P:(m + 1) * P], ident[:])
                last.then_inc(t_ready, 1)

        @block.scalar
        def _(act):
            def copy(o, i, scale=1.0):
                return nc.scalar.activation(o, i, ACT.Copy, scale=scale)

            def ready(i):
                act.wait_ge(t_ready, i + 1)
                return t_bank[:, i % 4, :]

            def free(ins, i):
                ins.then_inc(t_free[i % 4], 1)

            act_n = [0]

            def link(ins):
                act_n[0] += 1
                ins.then_inc(act_chain, 1)
                act.wait_ge(act_chain, act_n[0])

            def squares(n, used0, ready_wait):
                for k in range(n):
                    ready_wait(k)
                    if k >= 2:
                        act.wait_ge(sq_used, used0 + k - 1)
                    nc.scalar.activation(nring[:, k % 2, :], hT[:, k, :], ACT.Square).then_inc(sq_ready, 1)

            def root(i, e=0):
                b = ready(i)
                ins = nc.scalar.activation(rstd[:], b, ACT.Sqrt, bias=eps[:, e:e + 1], scale=1.0 / D)
                link(ins)
                act.nop().then_inc(t_free[i % 4], 1)
                act.nop().then_inc(std_ready, 1)

            def evac_pair(j, dst):
                act.wait_ge(w_used, j + 1)

            act.wait_ge(in_mem1, 16)
            act.wait_ge(in_small, 16 * sum(len(s) for s in PARAM_SETS))
            act.wait_ge(const_ready, 1)
            for m in range(MT):
                link(nc.scalar.activation(x_hi[:, 2 * m:2 * m + 2, :].rearrange("p a b -> p (a b)"), mem1[:, m, :], ACT.Square,
                                          accum_out=mstat[:, m:m + 1]))
            nc.scalar.activation(mstat[:, 2:4], mstat[:, 0:2], ACT.Sqrt, bias=eps[:, 0:1], scale=1.0 / D).then_inc(mem1_sq, 1)
            b = ready(0)
            c0 = 0
            for s in range(4):
                last = copy(cols[:, c0:c0 + SET_ROWS[s]], b[:, s * P:s * P + SET_ROWS[s]])
                c0 += SET_ROWS[s]
            free(last, 0)
            b = ready(1)
            link(copy(cols[:, c0:c0 + SET_ROWS[4]], b[:, 0:SET_ROWS[4]]))
            act.nop().then_inc(t_free[1], 1)
            act.nop().then_inc(cols_ready, 1)
            for i in range(4):
                b = ready(TASKS["mem1"] + i)
                for kk in range(2):
                    k = 2 * i + kk
                    copy(m_hi[:, k, :], b[:, kk * MEM:(kk + 1) * MEM], col["mem_norm"](k)).then_inc(m1_hi, 1)
            for k in range(DT):
                i = TASKS["x"] + k
                b = ready(i)
                copy(hT[:, k, :], b).then_inc(h_tile, 1)
                act.wait_ge(h_tile, k + 1)
                act.nop().then_inc(t_free[i % 4], 1)
            squares(DT, 0, lambda k: None)
            root(TASKS["stat1"])

            def norm_hi(base, k):
                act.wait_ge(nt_ready, base + k + 1)
                copy(x_hi[:, k, :], nring[:, k % 2, :]).then_inc(nhi_ready, 1)

            for i in range(4):
                norm_hi(0, 2 * i)
                norm_hi(0, 2 * i + 1)
                j = JOBS["kv1_k"] + i
                act.wait_ge(w_used, j + 1)
                copy(k1[:, 2 * i:2 * i + 2, :], g_bank[:, 2 * (j % 2):2 * (j % 2) + 2, 0:MEM]).then_inc(g_free[j % 2], 1)
            for i in range(4):
                j = JOBS["kv1_v"] + i
                act.wait_ge(w_used, j + 1)
                link(copy(v1[:, :, i * WC:(i + 1) * WC], g_bank[:, 2 * (j % 2), :].rearrange("p (m c) -> p m c", m=MT)))
                act.nop().then_inc(g_free[j % 2], 1)
                act.nop().then_inc(v1_ready, 1)

            act.wait_ge(pads, 1)
            act.wait_ge(in_bc, 48)
            link(nc.scalar.activation(bc[:, 1, :], bc[:, 1, :], ACT.Exp))

            def raw_pair(i, base):
                j = base + i
                act.wait_ge(w_used, j + 1)
                for f in range(2):
                    r = raw_n[0]
                    if r >= 2:
                        if r < XT + 2:
                            act.wait_ge(conv_ready, r - 1)
                        else:
                            act.wait_ge(d_ready, r - XT - 1)
                    last = copy(raw[:, f, PAD:PAD + T], g_bank[:, 2 * (j % 2) + f, :])
                    last.then_inc(raw_ready, 1)
                    raw_n[0] += 1
                act.wait_ge(raw_ready, raw_n[0])
                act.nop().then_inc(g_free[j % 2], 1)

            raw_n = [0]

            def silus(i):
                for f in range(2):
                    t = 2 * i + f
                    act.wait_ge(conv_ready, t + 1)
                    if t < XS:
                        dst = acc[:, f, 0:T]
                    elif t < XS + GROUPS:
                        dst = bT[:, t - XS, :]
                    else:
                        dst = cT[:, t - XS - GROUPS, :]
                    nc.scalar.activation(dst, acc[:, f, 0:T], ACT.Silu).then_inc(silu_ready, 1)

            def xbc_by_token(i):
                for f in range(2):
                    t = 2 * i + f
                    r = TASKS["xbcT"] + t
                    b = ready(r).rearrange("p (c q) -> p c q", c=CHUNKS)
                    if t < XS:
                        copy(xs01[:, :, t * P:(t + 1) * P], b[:, 0:2])
                        ins = copy(xs23[:, :, t * P:(t + 1) * P], b[:, 2:4])
                    else:
                        ins = copy(b_nat[:, :, (t - XS) * P:(t - XS + 1) * P], b)
                    link(ins)
                    act.nop().then_inc(t_free[r % 4], 1)
                    act.nop().then_inc(xs_ready, 1)

            for i in range(XT // 2):
                raw_pair(i, JOBS["xbc"])
                silus(i)
                if i:
                    xbc_by_token(i - 1)
            act.wait_ge(dtx, 1)
            nc.scalar.activation(t2[:], t2[:], ACT.Exp).then_inc(sp_e, 1)
            act.wait_ge(dtx, 2)
            nc.scalar.activation(cdec[:], t1[:], ACT.Ln).then_inc(sp_l, 1)
            raw_pair(0, JOBS["v"])

            def d_split(g):
                for f in range(2):
                    k = 2 * g + f
                    act.wait_ge(d_ready, k + 1)
                    copy(y_hi[:, k, :], acc[:, f, PAD:PAD + T]).then_inc(d_hi, 1)

            d_split(0)
            raw_pair(1, JOBS["v"])
            d_split(1)
            act.wait_ge(ac_ready, 1)
            nc.scalar.activation(eacs[:], acs[:], ACT.Exp)
            nc.scalar.activation(dtd[:], dtd[:], ACT.Exp)
            nc.scalar.activation(cdec[:], cdec[:], ACT.Exp).then_inc(ac_exp, 1)
            raw_pair(2, JOBS["v"])
            d_split(2)
            raw_pair(3, JOBS["v"])
            d_split(3)
            def decay(c):
                act.wait_ge(diff_ready, c + 1)
                nc.scalar.activation(m_[:], m_[:], ACT.Exp).then_inc(seg_ready, 1)

            for i in range(4):
                if i == 2:
                    decay(0)
                j = JOBS["z"] + i
                act.wait_ge(w_used, j + 1)
                for b in range(2):
                    ins = nc.scalar.activation(zs[:, 2 * b:2 * b + 2, i * WC:(i + 1) * WC],
                                               g_bank[:, 2 * (j % 2) + b, :].rearrange("p (m c) -> p m c", m=2), ACT.Silu)
                link(ins)
                act.nop().then_inc(g_free[j % 2], 1)
                act.nop().then_inc(zs_ready, 1)
            j = JOBS["pool"]
            for g in range(4):
                act.wait_ge(pool_group, g + 1)
                for f in range(2):
                    copy(y_hi[:, 2 * g + f, :], g_bank[:, 2 * ((j + 1 + g) % 2) + f, :], col["pool_scale"](2 * g + f)).then_inc(yp_hi, 1)
            for c in range(CHUNKS):
                act.wait_ge(y_ready, c + 1)
                link(nc.scalar.activation(xdd[:], y_nat[:], ACT.Square, accum_out=ysum[:, c, 0:1]))
                nc.scalar.activation(ysum[:, c, 1:2], ysum[:, c, 0:1], ACT.Sqrt, bias=eps[:, 0:1], scale=1.0 / SSD_INNER).then_inc(ysq_ready, 1)
                if c < CHUNKS - 1:
                    decay(c + 1)
                act.wait_ge(yr_ready, c + 1)
                copy(y_nat[:], y_nat[:], ysum[:, c, 0:1]).then_inc(yn_ready, 1)
                for g in range(2):
                    b = ready(TASKS[f"yT{c}"] + g)
                    for q in range(4):
                        k = 4 * g + q
                        copy(x_hi[:, k, c * P:(c + 1) * P], b[:, q * P:(q + 1) * P], col["ssd_norm"](k)).then_inc(ys_hi, 1)
            squares(DT, DT - 1, lambda k: act.wait_ge(h_done, 8 + k + 1))
            root(TASKS["stat2"])
            for k in range(DT):
                norm_hi(DT, k)
            for i in range(4):
                j = JOBS["q1"] + i
                act.wait_ge(w_used, j + 1)
                last = copy(qT[:, 2 * i:2 * i + 2, :], g_bank[:, 2 * (j % 2):2 * (j % 2) + 2, :])
                link(last)
                act.nop().then_inc(g_free[j % 2], 1)
                act.nop().then_inc(q_ready, 2)

            def p_T(m):
                for mm in range(MT):
                    i = TASKS[f"pT1_{m}"] + mm
                    b = ready(i)
                    copy(pT[:, mm, :, m * P:(m + 1) * P], b.rearrange("p (h q) -> p h q", h=XH_)).then_inc(pT_ready, 1)
                    act.wait_ge(pT_ready, 2 * m + mm + 1)
                    act.nop().then_inc(t_free[i % 4], 1)

            for m in range(TT):
                act.wait_ge(mx_ready, m + 1)
                if m >= 2:
                    act.wait_ge(t_ready, TASKS[f"pT1_{m - 2}"] + 2)
                for q in range(2):
                    i = TASKS[f"s1_{m}"] + q
                    b = ready(i)
                    for s in range(2):
                        h = 2 * q + s
                        last = nc.scalar.activation(pr[:, m % 2, h, :], b[:, s * MEM:(s + 1) * MEM], ACT.Exp,
                                                    bias=sst[:, m, 1, h:h + 1], scale=1.0 / 16, accum_out=sst[:, m, 2, h:h + 1])
                    link(last)
                    act.nop().then_inc(t_free[i % 4], 1)
                act.nop().then_inc(e_ready, 1)
                if m:
                    p_T(m - 1)
            p_T(TT - 1)
            for i in range(8):
                b = ready(TASKS["pv1"] + i)
                copy(y_hi[:, i, :], b).then_inc(o_hi, 1)
            act.wait_ge(mvar, 1)
            nc.scalar.activation(mstat[:, 52:54], mstat[:, 52:54], ACT.Sqrt, bias=eps[:, 1:2]).then_inc(mvar_root, 1)
            for i in range(4):
                b = ready(TASKS["mem2"] + i)
                for kk in range(2):
                    k = 2 * i + kk
                    act.wait_ge(m2_t, k + 1)
                    copy(m_hi[:, k, :], m2ring[:, k % 2, :]).then_inc(m2_hi, 1)
            squares(DT, 2 * (DT - 1), lambda k: act.wait_ge(h_done, 16 + k + 1))
            root(TASKS["stat3"])
            for k in range(DT):
                norm_hi(2 * DT, k)

            def kv(layer, jk, jv):
                for i in range(2):
                    j = jk + i
                    act.wait_ge(w_used, j + 1)
                    link(copy(k_m[layer][:, 2 * i:2 * i + 2, :], g_bank[:, 2 * (j % 2):2 * (j % 2) + 2, 0:MEM]))
                    act.nop().then_inc(g_free[j % 2], 1)
                for i in range(2):
                    j = jv + i
                    act.wait_ge(w_used, j + 1)
                    link(copy(v_m[layer][:, :, i * WC:(i + 1) * WC], g_bank[:, 2 * (j % 2), :].rearrange("p (m c) -> p m c", m=MT)))
                    act.nop().then_inc(g_free[j % 2], 1)
                act.nop().then_inc(kv_ready, 1)

            kv(0, JOBS["kva_k"], JOBS["kva_v"])
            f0 = 0
            for c, n in enumerate(FF_CHUNKS):
                with act.Fori(0, n // 2) as t:
                    for i in range(2):
                        tile = t * 2 + (f0 + i)
                        par = (JOBS[f"gu{c}"] + i) % 2
                        act.wait_ge(w_used, t * 2 + (JOBS[f"gu{c}"] + i + 1))
                        nc.scalar.activation(sg[:, i, :], g_bank[:, 2 * par, :], ACT.Silu).then_inc(sg_ready, 1)
                        act.wait_ge(ga_ready, tile + 1)
                        copy(y_hi[:, bass.ds(t * 2 + i, 1), :], ga[:, i:i + 1, :]).then_inc(ff_hi, 1)
                f0 += n
            squares(DT, 3 * (DT - 1), lambda k: act.wait_ge(h_done, 24 + 2 * 8 + k + 1))
            root(TASKS["stat4"])
            for k in range(DT):
                act.wait_ge(nt_ready, 3 * DT + k + 1)
                copy(x_hi[:, k, :], hT[:, k, :]).then_inc(nhi_ready, 1)
            kv(1, JOBS["kvb_k"], JOBS["kvb_v"])

            with act.Fori(0, CT_ // 2) as t:
                for i in range(2):
                    par = (JOBS["a_glu"] + i) % 2
                    act.wait_ge(w_used, t * 2 + (JOBS["a_glu"] + i + 1))
                    nc.scalar.activation(nring[:, i, :], g_bank[:, 2 * par + 1, :], ACT.Sigmoid).then_inc(glu_s, 1)

            def qm_evac(layer, i, base):
                j = base + i
                act.wait_ge(w_used, j + 1)
                link(copy(qmT[:, 2 * i:2 * i + 2, :], g_bank[:, 2 * (j % 2):2 * (j % 2) + 2, :]))
                act.nop().then_inc(g_free[j % 2], 1)
                act.nop().then_inc(qm_ready, 1)

            def gate_evac(j, tile):
                act.wait_ge(w_used, j + 1)
                link(nc.scalar.activation(gates[:, tile:tile + 2, :], g_bank[:, 2 * (j % 2):2 * (j % 2) + 2, :], ACT.Silu))
                act.nop().then_inc(g_free[j % 2], 1)
                act.nop().then_inc(gate_ready, 1)

            def mem_step(layer, n):
                if n >= 2 and n % 2 == 0:
                    m = n // 2 - 1
                    i = TASKS[f"mv{layer}_{m}"]
                    b = ready(i)
                    link(copy(qmT[:, :, m * P:(m + 1) * P], b.rearrange("p (h q) -> p h q", h=MH_)))
                    act.nop().then_inc(t_free[i % 4], 1)
                    act.nop().then_inc(mm_o, 1)
                if n < 8 and n % 2 == 0:
                    m = n // 2
                    act.wait_ge(mm_max, 4 * layer + m + 1)
                    if m:
                        act.wait_ge(t_ready, TASKS[f"mp{layer}_{m - 1}"] + 2)
                    for q in range(2):
                        i = TASKS[f"ms{layer}_{m}"] + q
                        b = ready(i)
                        for s in range(2):
                            h = 2 * q + s
                            last = nc.scalar.activation(prm[:, h, :], b[:, s * MEM:(s + 1) * MEM], ACT.Exp,
                                                        bias=mst[:, 4 * layer + m, 1, h:h + 1], scale=float(P) ** -0.5,
                                                        accum_out=mst[:, 4 * layer + m, 2, h:h + 1])
                        link(last)
                        act.nop().then_inc(t_free[i % 4], 1)
                    act.nop().then_inc(mm_exp, 1)
                if n % 2:
                    m = n // 2
                    for mm in range(MT):
                        i = TASKS[f"mp{layer}_{m}"] + mm
                        b = ready(i)
                        link(copy(pTm[:, mm], b.rearrange("p (h q) -> p h q", h=MH_)))
                        act.nop().then_inc(t_free[i % 4], 1)
                        act.nop().then_inc(mm_pT, 1)

            for i in range(2):
                qm_evac(0, i, JOBS["a_qm"])
            for n in range(8):
                gate_evac(JOBS["a_gate"] + n, (12 + 2 * n) % 16)
                mem_step(0, n)
            mem_step(0, 8)
            def mean_of(task, width):
                i = TASKS[task]
                b = ready(i)
                link(copy(mean[:], b, 1.0 / width))
                act.nop().then_inc(t_free[i % 4], 1)
                act.nop().then_inc(mean_ready, 1)

            def centred_squares(src, n, base, used0):
                for k in range(n):
                    act.wait_ge(cent_ready, base + k + 1)
                    if k >= 2:
                        act.wait_ge(csq_used, used0 + k - 1)
                    nc.scalar.activation(nring[:, k % 2, :], src(k), ACT.Square).then_inc(csq_ready, 1)

            def root_of(task, width):
                i = TASKS[task]
                b = ready(i)
                link(nc.scalar.activation(rstd[:], b, ACT.Sqrt, bias=eps[:, 1:2], scale=1.0 / width))
                act.nop().then_inc(t_free[i % 4], 1)
                act.nop().then_inc(root_ready, 1)

            mean_of("a_mean", CW)
            centred_squares(lambda k: hc[:, k, HP:HP + T], CT_, 0, 0)
            def y_part(k):
                act.wait_ge(yf_ready, (k + 4) % 16 + 1)
                if k < 8:
                    src, dst = gates[:, k, :], x_hi[:, k, :]
                elif k < CT_:
                    src, dst = hc[:, k, HP:HP + T], ya_hi[:, k - 8, :]
                else:
                    src, dst = qmT[:, k - CT_, :], ya_hi[:, k - 8, :]
                copy(dst, src).then_inc(yf_hi, 1)

            for k in range(CT_, 16):
                y_part(k)
            root_of("a_var", CW)
            for k in range(CT_):
                act.wait_ge(cn_ready, k + 1)
                nc.scalar.activation(hc[:, k, HP:HP + T], hc[:, k, HP:HP + T], ACT.Silu, bias=col["a_ln_b"](k),
                                     scale=col["a_ln_g"](k)).then_inc(cs_ready, 1)
                if k:
                    y_part(k - 1)
            y_part(CT_ - 1)

            def layer_norm(name, layer, last_norm):
                mean_of(f"mean_{name}", D)
                centred_squares(lambda k: hT[:, k, :], DT, CT_ + DT * layer, (CT_ - 1) + (DT - 1) * layer)
                root_of(f"var_{name}", D)
                for k in range(DT):
                    act.wait_ge(nt_ready, (4 + layer) * DT + k + 1)
                    if last_norm:
                        nc.scalar.activation(hT[:, k, :], hT[:, k, :], ACT.Identity, bias=col["b_post_b"](k)).then_inc(fin_ready, 1)
                    else:
                        nc.scalar.activation(x_hi[:, k, :], hT[:, k, :], ACT.Identity, bias=col["a_post_b"](k)).then_inc(nhi_ready, 1)

            layer_norm("a", 0, False)
            for n in range(2):
                j = JOBS["b_qi"] + n
                act.wait_ge(w_used, j + 1)
                link(copy(qiT[:, 2 * n:2 * n + 2, :], g_bank[:, 2 * (j % 2):2 * (j % 2) + 2, :]))
                act.nop().then_inc(g_free[j % 2], 1)
            j = JOBS["b_k"]
            act.wait_ge(w_used, j + 1)
            copy(kB[:], g_bank[:, 2 * (j % 2), :])
            link(copy(kiT[:], g_bank[:, 2 * (j % 2) + 1, :]))
            act.nop().then_inc(g_free[j % 2], 1)
            act.nop().then_inc(b_in, 1)
            j = JOBS["b_v"]
            act.wait_ge(w_used, j + 1)
            g = g_bank[:, 2 * (j % 2):2 * (j % 2) + 2, :].rearrange("p b (m c) -> p (b m) c", c=WC)
            copy(vB[:], g[:, :, 0:P])
            link(copy(wi[:], g[:, :, P:P + IH]))
            act.nop().then_inc(g_free[j % 2], 1)
            act.nop().then_inc(b_in, 2)
            for n in range(6):
                j = JOBS["b_q"] + n
                act.wait_ge(w_used, j + 1)
                link(copy(qB[:, 2 * n:2 * n + 2, :], g_bank[:, 2 * (j % 2):2 * (j % 2) + 2, :]))
                act.nop().then_inc(g_free[j % 2], 1)
                act.nop().then_inc(b_in, 1)
                for i in range(4 * n, 4 * n + 4):
                    qb = 1 + i // IH
                    r = TASKS["idx"] + i
                    b = ready(r)
                    if i >= 2:
                        act.wait_ge(acc_done, i - 1)
                    link(nc.scalar.activation(rring[:, i % 2, 0:W_OF[qb]], b[:, 0:W_OF[qb]], ACT.Relu))
                    act.nop().then_inc(t_free[r % 4], 1)
                    act.nop().then_inc(relu_ready, 1)

            def unit_step(u):
                if u:
                    qb, hg = UNITS[u - 1]
                    for kt in range(qb + 1):
                        i = TASKS[f"bT{u - 1}"] + kt
                        b = ready(i)
                        if kt == 0 and u > 1:
                            act.wait_ge(t_ready, TASKS[f"bV{u - 2}"] + 1)
                        link(copy(pTB[:, kt, :], b))
                        act.nop().then_inc(t_free[i % 4], 1)
                        act.nop().then_inc(uT_ready, 1)
                if u < len(UNITS):
                    for i in range(4):
                        act.wait_ge(um_ready, 4 * u + i + 1)
                        w = W_OF[UNITS[u][0]]
                        nc.scalar.activation(pB[:, i, 0:w], pB[:, i, 0:w], ACT.Exp, bias=ast[:, u, 0, i:i + 1],
                                             accum_out=ast[:, u, 1, i:i + 1]).then_inc(ue_ready, 1)
                if u:
                    qb, hg = UNITS[u - 1]
                    i = TASKS[f"bV{u - 1}"]
                    b = ready(i)
                    link(copy(qB[:, 4 * hg:4 * hg + 4, qb * P:(qb + 1) * P], b.rearrange("p (h q) -> p h q", h=4)))
                    act.nop().then_inc(t_free[i % 4], 1)
                    act.nop().then_inc(uo_ready, 1)

            for n in range(10):
                if n < 2:
                    qm_evac(1, n, JOBS["b_qm"])
                else:
                    gate_evac(JOBS["b_gate"] + n - 2, 2 * (n - 2))
                unit_step(n)
                if n >= 2:
                    mem_step(1, n - 2)
            for u in (10, 11, 12):
                unit_step(u)
            mem_step(1, 8)
            for k in range(16):
                act.wait_ge(yf_ready, 16 + k + 1)
                copy(x_hi[:, k, :] if k < 8 else yb_hi[:, k - 8, :], gates[:, k, :]).then_inc(yf_hi, 1)
            layer_norm("b", 1, True)
            for i in range(8):
                r = TASKS["out"] + i
                b = ready(r)
                if i >= 2:
                    act.wait_ge(out_done[i % 2], 16 * (i // 2))
                link(copy(onat[:, i % 2, :], b))
                act.nop().then_inc(t_free[r % 4], 1)
                act.nop().then_inc(on_ready, 1)

        @block.vector
        def _(dve):
            v = nc.vector
            chain = [0]

            def link(ins, behind=0):
                ins.then_inc(dve_chain, 1)
                chain[0] = chain[0] + 1
                dve.wait_ge(dve_chain, chain[0] - behind)

            def done(ins, *signals):
                link(ins)
                for s in signals:
                    dve.nop().then_inc(s, 1)

            def ready(i):
                dve.wait_ge(t_ready, i + 1)
                return t_bank[:, i % 4, :]

            def loop(n, per):
                start = chain[0]

                class Loop:
                    def __enter__(self):
                        self.f = dve.Fori(0, n)
                        t = self.f.__enter__()
                        chain[0] = t * per + start
                        return t

                    def __exit__(self, *e):
                        self.f.__exit__(*e)
                        chain[0] = start + n * per
                return Loop()

            def add_to_residual(base, n=4):
                for i in range(n):
                    j = base + i
                    dve.wait_ge(w_used, j + 1)
                    for f in range(2):
                        k = 2 * i + f
                        ins = v.tensor_tensor(hT[:, k, :], hT[:, k, :], g_bank[:, 2 * (j % 2) + f, :], ALU.add)
                        if f == 0:
                            ins.then_inc(h_done, 1)
                        else:
                            done(ins, h_done, g_free[j % 2])

            def rms_apply(nth, gain):
                base = nth * DT
                dve.wait_ge(std_ready, nth + 1)
                link(v.reciprocal(rstd[:], rstd[:]))
                for k in range(DT):
                    if k >= 2:
                        dve.wait_ge(nlo_ready, base + k - 1)
                    v.scalar_tensor_tensor(nring[:, k % 2, :], hT[:, k, :], gain(k), rstd[:], ALU.mult, ALU.mult).then_inc(nt_ready, 1)
                    if k:
                        rms_lo(base, k - 1)
                rms_lo(base, DT - 1)

            def rms_lo(base, k):
                dve.wait_ge(nhi_ready, base + k + 1)
                v.tensor_tensor(x_lo[:, k, :], nring[:, k % 2, :], x_hi[:, k, :].bitcast(F32), ALU.subtract).then_inc(nlo_ready, 1)

            dve.wait_ge(mem1_sq, 1)
            link(v.reciprocal(mstat[:, 4:6], mstat[:, 2:4]))
            for m in range(MT):
                v.tensor_scalar(mem1[:, m, :], mem1[:, m, :], mstat[:, 4 + m:5 + m], None, ALU.mult).then_inc(mem1_n, 1)
            dve.wait_ge(cols_ready, 1)
            for i in range(4):
                r = TASKS["mem1"] + i
                b = ready(r)
                for kk in range(2):
                    k = 2 * i + kk
                    dve.wait_ge(m1_hi, 2 * i + 2)
                    ins = v.scalar_tensor_tensor(m_lo[:, k, :], b[:, kk * MEM:(kk + 1) * MEM], col["mem_norm"](k),
                                                 m_hi[:, k, :].bitcast(F32), ALU.mult, ALU.subtract)
                    done(ins, m1_lo, *([t_free[r % 4]] * kk))
            dve.wait_ge(t_ready, TASKS["x"] + DT)
            for b in (raw, acc):
                ins = v.memset(b[:, :, 0:PAD], 0.0)
            done(ins, pads)
            dve.wait_ge(h_tile, DT)
            rms_apply(0, col["mix_norm"])

            for t in range(XT):
                f = t % 2
                dve.wait_ge(raw_ready, t + 1)
                if t >= 2:
                    dve.wait_ge(silu_ready, t - 1)
                    if t - 2 < XS:
                        dve.wait_ge(t_ready, TASKS["xbcT"] + t - 2 + 1)
                w = lambda k: col["conv_w"](k * XT + t)
                s = lambda k: raw[:, f, PAD - 3 + k:PAD - 3 + k + T]
                link(v.tensor_scalar(acc[:, f, 0:T], s(3), w(3), col["conv_b"](t), ALU.mult, ALU.add))
                for k in (2, 1):
                    link(v.scalar_tensor_tensor(acc[:, f, 0:T], s(k), w(k), acc[:, f, 0:T], ALU.mult, ALU.add))
                v.scalar_tensor_tensor(acc[:, f, 0:T], s(0), w(0), acc[:, f, 0:T], ALU.mult, ALU.add).then_inc(conv_ready, 1)
            j = JOBS["dt"]
            dve.wait_ge(w_used, j + 1)
            g = g_bank[:, 2 * (j % 2):2 * (j % 2) + 2, :].rearrange("p b (m c) -> p (b m) c", c=WC)[:, :, 0:HEADS]
            done(v.tensor_tensor(t3[:], g, bc[:, 0:1, :].to_broadcast([P, CHUNKS, HEADS]), ALU.add), g_free[j % 2])
            v.scalar_tensor_tensor(t2[:], t3[:], -1.0, t3[:], ALU.mult, ALU.min).then_inc(dtx, 1)
            dve.wait_ge(sp_e, 1)
            link(v.tensor_scalar(t1[:], t2[:], 1.0, None, ALU.add))
            dve.nop().then_inc(dtx, 1)
            link(v.scalar_tensor_tensor(acs[:], t1[:], -1.0, t2[:], ALU.add, ALU.subtract))
            link(v.reciprocal(eacs[:], t1[:]))
            link(v.tensor_tensor(dtd[:], acs[:], eacs[:], ALU.mult))
            dve.wait_ge(sp_l, 1)
            link(v.scalar_tensor_tensor(dt_[:], t3[:], 0.0, cdec[:], ALU.max, ALU.add))
            link(v.tensor_tensor(dt_[:], dt_[:], dtd[:], ALU.subtract))
            v.scalar_tensor_tensor(adt[:], dt_[:], -1.0, bc[:, 1:2, :].to_broadcast([P, CHUNKS, HEADS]),
                                   ALU.mult, ALU.mult).then_inc(adt_ready, 1)

            def window(i):
                w = WINDOWS[i]
                for f in range(2):
                    k = 2 * i + f
                    dve.wait_ge(raw_ready, XT + k + 1)
                    if k < 2:
                        if k == 0:
                            link(v.memset(wbuf[:, :, 0:PAD], 0.0))
                        dve.wait_ge(silu_ready, XT)
                        link(v.memset(acc[:, f, 0:PAD], 0.0))
                    src, s = raw, 1
                    bufs = {1: (acc,), 2: (wbuf, acc), 3: (acc, wbuf, acc), 4: (wbuf, acc, wbuf, acc)}[i + 1]
                    for b in bufs:
                        link(v.tensor_tensor(b[:, f, PAD:PAD + T], src[:, f, PAD:PAD + T], src[:, f, PAD - s:PAD - s + T], ALU.add))
                        src, s = b, 2 * s
                    a, r = acc[:, f, PAD:PAD + T], raw[:, f, PAD:PAD + T]
                    link(v.tensor_tensor(a[:, 0:16], a[:, 0:16], inv_n[:, i, :], ALU.mult))
                    v.tensor_tensor(a[:, 0:16], a[:, 0:16], r[:, 0:16], ALU.subtract)
                    v.scalar_tensor_tensor(a[:, 16:T], a[:, 16:T], 1.0 / w, r[:, 16:T], ALU.mult, ALU.subtract).then_inc(d_ready, 1)
                for f in range(2):
                    k = 2 * i + f
                    dve.wait_ge(d_hi, k + 1)
                    v.tensor_tensor(y_lo[:, k, :], acc[:, f, PAD:PAD + T], y_hi[:, k, :].bitcast(F32), ALU.subtract).then_inc(d_lo, 1)
                dve.wait_ge(d_lo, 2 * i + 2)

            def bcast(t, c, n):
                return t[:, c, :].unsqueeze(2).to_broadcast([P, HEADS, n])

            window(0)
            r = TASKS["acs"]
            b = ready(r)
            fl = "p c h -> p (c h)"
            link(v.tensor_copy(acs[:].rearrange(fl), b[:, 0:64]))
            v.tensor_tensor(dtd[:].rearrange(fl), b[:, 64:128], acs[:].rearrange(fl), ALU.subtract)
            done(v.tensor_copy(cdec[:].rearrange(fl), b[:, 64:128]), t_free[r % 4], ac_ready)
            window(1)
            dve.wait_ge(ac_exp, 1)
            link(v.tensor_tensor(dtd[:], dtd[:], dt_[:], ALU.mult))
            window(2)
            window(3)
            for i in range(2):
                r = TASKS["cb"] + i
                b = ready(r).rearrange("p (c q) -> p c q", c=4)
                v.tensor_tensor(cbm[:, 2 * i:2 * i + 2].rearrange("p c g q -> p (c g) q"), b,
                                tri[:].unsqueeze(1).to_broadcast([P, 4, P]), ALU.mult).then_inc(t_free[r % 4], 1)

            def diff(c):
                for q in range(4):
                    r = TASKS[f"abc{c}"] + q
                    b = ready(r)
                    for i in range(4):
                        h = 4 * q + i
                        ins = v.tensor_scalar(m_[:, h, :], b[:, i * P:(i + 1) * P], acs[:, c, h:h + 1], 0.0, ALU.subtract, ALU.min)
                    if q < 3:
                        ins.then_inc(t_free[r % 4], 1)
                    else:
                        done(ins, t_free[r % 4], diff_ready)

            diff(0)
            def chunk_inputs(c):
                xv = xs_nat(c).rearrange("p (h d) -> p h d", h=HEADS)
                if c == 0:
                    dve.wait_ge(xs_ready, XS + GROUPS)
                ins = v.tensor_tensor(xdt[:], xv, bcast(dt_, c, HD), ALU.mult)
                if c < CHUNKS - 1:
                    ins = v.tensor_tensor(xdd[:], xv, bcast(dtd, c, HD), ALU.mult)
                ins.then_inc(xdt_ready, 1)
                dve.wait_ge(seg_ready, c + 1)
                for g in range(GROUPS):
                    ms = m_[:, g * HPG:(g + 1) * HPG, :]
                    ins = v.tensor_tensor(ms, ms, cbm[:, c, g, :].unsqueeze(1).to_broadcast([P, HPG, P]), ALU.mult)
                ins.then_inc(m_ready, 1)

            chunk_inputs(0)
            j = JOBS["pool"]
            for k in range(8):
                dve.wait_ge(yp_hi, k + 1)
                ins = v.scalar_tensor_tensor(y_lo[:, k, :], g_bank[:, 2 * ((j + 1 + k // 2) % 2) + k % 2, :], col["pool_scale"](k),
                                             y_hi[:, k, :].bitcast(F32), ALU.mult, ALU.subtract)
                done(ins, yp_lo, *([g_free[j % 2]] * (k == 7)))
            for c in range(CHUNKS):
                xv = xs_nat(c).rearrange("p (h d) -> p h d", h=HEADS)
                halves = [slice(g * HPG, (g + 1) * HPG) for g in range(2)]
                if c:
                    dve.wait_ge(t_ready, TASKS[f"yT{c - 1}"] + 2)
                    for g in range(2):
                        r = TASKS[f"yoff{c}"] + g
                        b = ready(r).rearrange("p (h d) -> p h d", h=HPG)
                        v.tensor_tensor(y_nat[:, halves[g], :], b, eacs[:, c, halves[g]].unsqueeze(2).to_broadcast([P, HPG, HD]),
                                        ALU.mult).then_inc(t_free[r % 4], 1)
                    if c < CHUNKS - 1:
                        link(v.tensor_tensor(prev[:], prev[:], bcast(cdec, c, HD), ALU.mult))
                if c < CHUNKS - 1:
                    for g in range(2):
                        r = TASKS[f"state{c}"] + g
                        b = ready(r).rearrange("p (h d) -> p h d", h=HPG)
                        if c == 0:
                            ins = v.tensor_copy(prev[:, halves[g], :], b)
                        else:
                            ins = v.tensor_tensor(prev[:, halves[g], :], prev[:, halves[g], :], b, ALU.add)
                        if g == 0:
                            ins.then_inc(t_free[r % 4], 1)
                        else:
                            done(ins, t_free[r % 4], prev_ready)
                link(v.tensor_tensor(xdd[:], xv, bc[:, 2, :].unsqueeze(2).to_broadcast([P, HEADS, HD]), ALU.mult))
                for g in range(2):
                    r = TASKS[f"ydiag{c}"] + g
                    b = ready(r).rearrange("p (h d) -> p h d", h=HPG)
                    other = y_nat if c else xdd
                    ins = v.tensor_tensor(y_nat[:, halves[g], :], other[:, halves[g], :], b, ALU.add)
                    if g == 0:
                        ins.then_inc(t_free[r % 4], 1)
                    else:
                        done(ins, t_free[r % 4])
                if c:
                    link(v.tensor_tensor(y_nat[:], y_nat[:], xdd[:], ALU.add))
                dve.wait_ge(zs_ready, 4)
                v.tensor_tensor(y_nat[:], y_nat[:], zs[:, c, :].rearrange("p (h d) -> p h d", h=HEADS), ALU.mult).then_inc(y_ready, 1)
                if c < CHUNKS - 1:
                    diff(c + 1)
                dve.wait_ge(ysq_ready, c + 1)
                v.reciprocal(ysum[:, c, 0:1], ysum[:, c, 1:2]).then_inc(yr_ready, 1)
                if c < CHUNKS - 1:
                    chunk_inputs(c + 1)
                j = JOBS["wo_pool"] + c
                dve.wait_ge(w_used, j + 1)
                for f in range(2):
                    k = 2 * c + f
                    ins = v.tensor_tensor(hT[:, k, :], hT[:, k, :], g_bank[:, 2 * (j % 2) + f, :], ALU.add)
                    if f == 0:
                        ins.then_inc(h_done, 1)
                    else:
                        done(ins, h_done, g_free[j % 2])
                for g in range(2):
                    r = TASKS[f"yT{c}"] + g
                    b = ready(r)
                    for q in range(4):
                        k = 4 * g + q
                        dve.wait_ge(ys_hi, 8 * c + 4 * g + 4)
                        ins = v.scalar_tensor_tensor(x_lo[:, k, c * P:(c + 1) * P], b[:, q * P:(q + 1) * P], col["ssd_norm"](k),
                                                     x_hi[:, k, c * P:(c + 1) * P].bitcast(F32), ALU.mult, ALU.subtract)
                        if q < 3:
                            ins.then_inc(ys_lo, 1)
                        else:
                            done(ins, ys_lo, t_free[r % 4])
            add_to_residual(JOBS["wo_ssd"])
            rms_apply(1, col["xattn_norm"])

            def scores_max(m):
                for q in range(2):
                    b = ready(TASKS[f"s1_{m}"] + q).rearrange("p (h k) -> p h k", h=2)
                    ins = v.reduce_max(sst[:, m, 0, 2 * q:2 * q + 2], b, AX.X)
                link(ins)
                v.tensor_scalar(sst[:, m, 1, :], sst[:, m, 0, :], -1.0 / 16, None, ALU.mult).then_inc(mx_ready, 1)

            scores_max(0)
            for m in range(TT):
                if m < TT - 1:
                    scores_max(m + 1)
                dve.wait_ge(e_ready, m + 1)
                link(v.reciprocal(sst[:, m, 3, :], sst[:, m, 2, :]))
                for h in range(XH_):
                    ins = v.tensor_scalar(pr[:, m % 2, h, :], pr[:, m % 2, h, :], sst[:, m, 3, h:h + 1], None, ALU.mult)
                ins.then_inc(p_ready, 1)
            for i in range(8):
                r = TASKS["pv1"] + i
                b = ready(r)
                dve.wait_ge(o_hi, i + 1)
                done(v.tensor_tensor(y_lo[:, i, :], b, y_hi[:, i, :].bitcast(F32), ALU.subtract), o_lo, t_free[r % 4])
            dve.wait_ge(in_mem2, 16)
            for m in range(MT):
                for h in range(2):
                    link(v.bn_stats(mstat[:, 8 + 12 * m + 6 * h:14 + 12 * m + 6 * h], mem2[:, m, h * 512:(h + 1) * 512]))
                link(v.bn_aggr(mstat[:, 40 + 2 * m:42 + 2 * m], mstat[:, 8 + 12 * m:20 + 12 * m].rearrange("p (a b) -> p a b", a=2)))
                link(v.tensor_copy(mstat[:, 52 + m:53 + m], mstat[:, 41 + 2 * m:42 + 2 * m]))
            dve.nop().then_inc(mvar, 1)
            dve.wait_ge(mvar_root, 1)
            link(v.reciprocal(mstat[:, 54:56], mstat[:, 52:54]))
            for m in range(MT):
                v.tensor_scalar(mem2[:, m, :], mem2[:, m, :], mstat[:, 40 + 2 * m:41 + 2 * m], mstat[:, 54 + m:55 + m],
                                ALU.subtract, ALU.mult).then_inc(mem2_n, 1)
            def m2_lo_part(k):
                dve.wait_ge(m2_hi, k + 1)
                v.tensor_tensor(m_lo[:, k, :], m2ring[:, k % 2, :], m_hi[:, k, :].bitcast(F32), ALU.subtract).then_inc(m2_lo, 1)

            for k in range(DT):
                r = TASKS["mem2"] + k // 2
                b = ready(r)[:, k % 2 * MEM:(k % 2 + 1) * MEM]
                done(v.tensor_scalar(m2ring[:, k % 2, :], b, col["mem_ln_g"](k), col["mem_ln_b"](k), ALU.mult, ALU.add),
                     m2_t, *([t_free[r % 4]] * (k % 2)))
                m2_lo_part(k)
            add_to_residual(JOBS["wo1"])

            rms_apply(2, col["ffn_norm"])
            f0 = 0
            for c, n in enumerate(FF_CHUNKS):
                with loop(n // 2, 2) as t:
                    for i in range(2):
                        par = (JOBS[f"gu{c}"] + i) % 2
                        tile = t * 2 + (f0 + i + 1)
                        dve.wait_ge(sg_ready, tile)
                        done(v.tensor_tensor(ga[:, i, :], sg[:, i, :], g_bank[:, 2 * par + 1, :], ALU.mult), ga_ready, g_free[par])
                        dve.wait_ge(ff_hi, tile)
                        d = bass.ds(t * 2 + i, 1)
                        v.tensor_tensor(y_lo[:, d, :], ga[:, i:i + 1, :], y_hi[:, d, :].bitcast(F32), ALU.subtract).then_inc(ff_lo, 1)
                f0 += n
                add_to_residual(JOBS[f"down{c}"])
            def final_lo(k):
                dve.wait_ge(nhi_ready, 3 * DT + k + 1)
                v.tensor_tensor(x_lo[:, k, :], hT[:, k, :], x_hi[:, k, :].bitcast(F32), ALU.subtract).then_inc(nlo_ready, 1)

            dve.wait_ge(std_ready, 4)
            link(v.reciprocal(rstd[:], rstd[:]))
            for k in range(DT):
                v.scalar_tensor_tensor(hT[:, k, :], hT[:, k, :], col["final_norm"](k), rstd[:], ALU.mult, ALU.mult).then_inc(nt_ready, 1)
                if k:
                    final_lo(k - 1)
            final_lo(DT - 1)


            done(v.memset(hc[:, :, 0:HP], 0.0))

            def gated(tile, i):
                par = (JOBS["a_glu"] + i) % 2
                dve.wait_ge(glu_s, tile + 1)
                done(v.tensor_tensor(hc[:, bass.ds(tile, 1), HP:HP + T], g_bank[:, 2 * par:2 * par + 1, :], nring[:, i:i + 1, :],
                                     ALU.mult), g_free[par])

            def taps(tile, k0, k1):
                if isinstance(tile, int):
                    h = lambda k: hc[:, tile, k:k + T]
                    w = lambda c: cols[:, c + tile:c + tile + 1]
                    a = lambda k: cacc[:, k % 2, :]
                else:
                    h = lambda k: hc[:, bass.ds(tile, 1), k:k + T]
                    w = lambda c: cols[:, bass.ds(tile + c, 1)]
                    a = lambda k: cacc[:, k % 2:k % 2 + 1, :]
                for k in range(k0, k1):
                    wk = w(COL["a_conv_w0"] + k * CT_)
                    if k == 0:
                        ins = v.tensor_scalar(a(k), h(k), wk, w(COL["a_conv_b"]), ALU.mult, ALU.add)
                    elif k == 1:
                        ins = v.tensor_scalar(a(k), h(k), wk, 0.0, ALU.mult, ALU.add)
                    else:
                        ins = v.scalar_tensor_tensor(a(k), h(k), wk, a(k), ALU.mult, ALU.add)
                    link(ins, 0 if k in (k1 - 1, TAPS - 1) else 1)
                if k1 == TAPS:
                    done(v.tensor_tensor(h(TAPS - 1), a(0), a(1), ALU.add), conv_done)

            with loop(CT_ // 2, TAPS + 3) as t:
                gated(t * 2, 0)
                taps(t, 0, 16)
                gated(t * 2 + 1, 1)
                taps(t, 16, TAPS)

            def mem_max(layer, m):
                for q in range(2):
                    b = ready(TASKS[f"ms{layer}_{m}"] + q).rearrange("p (h k) -> p h k", h=2)
                    ins = v.reduce_max(mst[:, 4 * layer + m, 0, 2 * q:2 * q + 2], b, AX.X)
                link(ins)
                v.tensor_scalar(mst[:, 4 * layer + m, 1, :], mst[:, 4 * layer + m, 0, :], -float(P) ** -0.5, None, ALU.mult).then_inc(mm_max, 1)

            def mem_prob(layer, m):
                dve.wait_ge(mm_exp, 4 * layer + m + 1)
                link(v.reciprocal(mst[:, 4 * layer + m, 3, :], mst[:, 4 * layer + m, 2, :]))
                for h in range(MH_):
                    ins = v.tensor_scalar(prm[:, h, :], prm[:, h, :], mst[:, 4 * layer + m, 3, h:h + 1], None, ALU.mult)
                ins.then_inc(mm_prob, 1)

            for i in range(CT_ // 2):
                tile = CT_ // 2 + i
                if 1 <= i <= TT:
                    mem_max(0, i - 1)
                taps(tile, 0, 8)
                if 1 <= i <= TT:
                    mem_prob(0, i - 1)
                taps(tile, 8, TAPS)
            dve.wait_ge(mean_ready, 1)
            for k in range(CT_):
                c = hc[:, k, HP:HP + T]
                v.tensor_tensor(c, c, mean[:], ALU.subtract).then_inc(cent_ready, 1)

            def y_product(k):
                if k < CT_:
                    dve.wait_ge(cs_ready, k + 1)
                if k == CT_:
                    dve.wait_ge(mm_o, TT)
                    dve.wait_ge(gate_ready, 8)
                a = hc[:, k, HP:HP + T] if k < CT_ else qmT[:, k - CT_, :]
                v.tensor_tensor(gates[:, k, :] if k < 8 else a, a, gates[:, k, :], ALU.mult).then_inc(yf_ready, 1)

            def y_rest(k):
                dve.wait_ge(yf_hi, (k + 4) % 16 + 1)
                if k < 8:
                    src, hi, lo = gates[:, k, :], x_hi[:, k, :], x_lo[:, k, :]
                elif k < CT_:
                    src, hi, lo = hc[:, k, HP:HP + T], ya_hi[:, k - 8, :], ya_lo[:, k - 8, :]
                else:
                    src, hi, lo = qmT[:, k - CT_, :], ya_hi[:, k - 8, :], ya_lo[:, k - 8, :]
                v.tensor_tensor(lo, src, hi.bitcast(F32), ALU.subtract).then_inc(yf_lo, 1)

            for k in range(CT_, 16):
                y_product(k)
                if k > CT_:
                    y_rest(k - 1)
            y_rest(15)
            dve.wait_ge(root_ready, 1)
            link(v.reciprocal(rstd[:], rstd[:]))
            for k in range(CT_ + 2):
                if k < CT_:
                    c = hc[:, k, HP:HP + T]
                    v.tensor_tensor(c, c, rstd[:], ALU.mult).then_inc(cn_ready, 1)
                if 1 <= k < CT_ + 1:
                    y_product(k - 1)
                if k >= 2:
                    y_rest(k - 2)

            def add_out(base):
                for half in range(2):
                    for i in range(4):
                        j = base + 4 * half + i
                        dve.wait_ge(w_used, j + 1)
                        for f in range(2):
                            k = 2 * i + f
                            ins = v.scalar_tensor_tensor(hT[:, k, :], hT[:, k, :], 1.0 if half else ALPHA,
                                                         g_bank[:, 2 * (j % 2) + f, :], ALU.mult, ALU.add)
                            if f == 0:
                                ins.then_inc(h_done, 1)
                            else:
                                done(ins, h_done, g_free[j % 2])

            def layer_norm(layer, gain, bias, last_norm):
                dve.wait_ge(mean_ready, 2 + layer)
                for k in range(DT):
                    v.tensor_tensor(hT[:, k, :], hT[:, k, :], mean[:], ALU.subtract).then_inc(cent_ready, 1)
                dve.wait_ge(root_ready, 2 + layer)
                link(v.reciprocal(rstd[:], rstd[:]))
                def lo_part(k):
                    dve.wait_ge(nhi_ready, 4 * DT + k + 1)
                    v.scalar_tensor_tensor(x_lo[:, k, :], hT[:, k, :], bias(k), x_hi[:, k, :].bitcast(F32),
                                           ALU.add, ALU.subtract).then_inc(nlo_ready, 1)

                for k in range(DT):
                    v.scalar_tensor_tensor(hT[:, k, :], hT[:, k, :], gain(k), rstd[:], ALU.mult, ALU.mult).then_inc(nt_ready, 1)
                    if k and not last_norm:
                        lo_part(k - 1)
                if not last_norm:
                    lo_part(DT - 1)
                    dve.wait_ge(nlo_ready, 5 * DT)
                    for k in range(DT):
                        ins = v.tensor_scalar(hT[:, k, :], hT[:, k, :], bias(k), None, ALU.add)
                    link(ins)

            add_out(JOBS["a_out"])
            layer_norm(0, col["a_post_g"], col["a_post_b"], False)
            dve.wait_ge(dist_ready, 1)
            link(v.tensor_scalar(dist[:], dist_i[:], 0.0, None, ALU.add))
            link(v.scalar_tensor_tensor(dist[:], dist[:], -1.0, dist[:], ALU.mult, ALU.max))
            link(v.memset(mask[:, 0:P], 0.0))
            link(v.memset(mask[0:64, 64:P], NEG))
            dve.wait_ge(b_in, 3)

            def indexer(qb):
                for h in range(IH):
                    i = (qb - 1) * IH + h
                    s = isc[:, I_AT[qb]:I_AT[qb] + W_OF[qb]]
                    dve.wait_ge(relu_ready, i + 1)
                    r = rring[:, i % 2, 0:W_OF[qb]]
                    if h == 0:
                        ins = v.tensor_scalar(s, r, wi[:, qb, h:h + 1], 0.0, ALU.mult, ALU.add)
                    else:
                        ins = v.scalar_tensor_tensor(s, r, wi[:, qb, h:h + 1], s, ALU.mult, ALU.add)
                    ins.then_inc(acc_done, 1)
                    dve.wait_ge(acc_done, i + 1)

            def top_k(qb):
                w = W_OF[qb]
                s = isc[:, I_AT[qb]:I_AT[qb] + w]
                link(v.memset(s[0:64, w - 64:w], NEG))
                for _ in range(TOPK // 8):
                    link(v.max(m8[:], s))
                    link(v.match_replace(s, m8[:], s, TAKEN))
                link(v.tensor_scalar(mask[:, M_AT[qb]:M_AT[qb] + w], s, TAKEN, NEG, ALU.is_gt, ALU.mult))

            for qb in range(1, TT):
                indexer(qb)
                top_k(qb)

            def unit(u):
                qb, hg = UNITS[u]
                w = W_OF[qb]
                if u:
                    dve.wait_ge(t_ready, TASKS[f"bT{u - 1}"] + UNITS[u - 1][0] + 1)
                for i in range(4):
                    h = 4 * hg + i
                    r = TASKS[f"bL{u}"] + i
                    p = pB[:, i, 0:w]
                    link(v.scalar_tensor_tensor(p, dist[:, T - w:T], -SLOPES[h], mask[:, M_AT[qb]:M_AT[qb] + w], ALU.mult, ALU.add))
                    b = ready(r)
                    done(v.scalar_tensor_tensor(p, b[:, 0:w], float(P) ** -0.5, p, ALU.mult, ALU.add), t_free[r % 4])
                    v.tensor_reduce(ast[:, u, 0, i:i + 1], p, AX.X, ALU.max, negate=True).then_inc(um_ready, 1)

            def unit_prob(u):
                w = W_OF[UNITS[u][0]]
                dve.wait_ge(ue_ready, 4 * u + 4)
                link(v.reciprocal(ast[:, u, 2, :], ast[:, u, 1, :]))
                for i in range(4):
                    ins = v.tensor_scalar(pB[:, i, 0:w], pB[:, i, 0:w], ast[:, u, 2, i:i + 1], None, ALU.mult)
                ins.then_inc(up_ready, 1)

            for n in range(12):
                unit(n)
                unit_prob(n)
                if 2 <= n < 10:
                    (mem_prob if n % 2 else mem_max)(1, (n - 2) // 2)
            for k in range(17):
                if k < 16:
                    if k == 0:
                        dve.wait_ge(uo_ready, 12)
                        dve.wait_ge(gate_ready, 16)
                    if k == AH:
                        dve.wait_ge(mm_o, 2 * TT)
                    a = qB[:, k, :] if k < AH else qmT[:, k - AH, :]
                    v.tensor_tensor(gates[:, k, :], gates[:, k, :], a, ALU.mult).then_inc(yf_ready, 1)
                if k:
                    q = k - 1
                    dve.wait_ge(yf_hi, 16 + k)
                    lo, hi = (x_lo[:, q, :], x_hi[:, q, :]) if q < 8 else (yb_lo[:, (q - 4) % 8, :], yb_hi[:, q - 8, :])
                    v.tensor_tensor(lo, gates[:, q, :], hi.bitcast(F32), ALU.subtract).then_inc(yf_lo, 1)
            add_out(JOBS["b_out"])
            layer_norm(1, col["b_post_g"], col["b_post_b"], True)


_NAMES = ["x", "mem", "mix_norm", "w_in", "conv_w", "conv_b", "dt_bias", "a_log", "d_skip", "ssd_norm", "pool_w",
          "pool_scale", "w_out_mix", "xattn_norm", "mem_norm", "w_q", "w_kv", "w_o", "ffn_norm", "w_gate_up", "w_down",
          "final_norm", "mem_2", "mem_ln_g_2", "mem_ln_b_2", "a_w_in_2", "a_conv_w_2", "a_conv_b_2", "a_ln_g_2",
          "a_ln_b_2", "a_w_mkv_2", "a_w_out_2", "a_post_g_2", "a_post_b_2", "b_w_in_2", "b_w_mkv_2", "b_w_out_2",
          "b_post_g_2", "b_post_b_2"]


def kernel(**inputs):
    import concourse.bacc as _bacc
    from concourse.bass_utils import run_bass_kernel_spmd as _run

    nc = _bacc.Bacc("TRN2", target_bir_lowering=False, num_devices=1, dynamic_dma_scratch_size=1024)
    arrays, aps = {}, {}
    for name in _NAMES:
        arrays[name] = np.ascontiguousarray(inputs[name])
        aps[name] = nc.dram_tensor(name, arrays[name].shape, F32, kind="ExternalInput").ap()
    out = nc.dram_tensor("out", (1, T, D), F32, kind="ExternalOutput").ap()
    program(nc, aps, out)
    r = _run(nc, [arrays], core_ids=[0])
    return r.results[0]["out"]
```
